# Optimizing a Trainium2 kernel written in Bass

```python
import math
import jax, jax.numpy as jnp
from jax import lax
import numpy as np

D_MODEL = 1024
BATCH = 1
SEQ = 256
DEPTH = 2

N_MIXERS = 2
N_POOL_LAYERS = (DEPTH + 1) // 2
N_ATTN_LAYERS = DEPTH // 2
ALPHA = (2.0 * DEPTH) ** 0.25
BETA = (8.0 * DEPTH) ** -0.25
LN_EPS = 1e-5
POOL_WINDOWS = (2, 4, 8, 16)
N_GROUPS = len(POOL_WINDOWS)
GROUP_W = D_MODEL // N_GROUPS
HEAD_DIM = 64
N_HEADS = D_MODEL // (2 * HEAD_DIM)
V_DIM = 2 * HEAD_DIM
D_ATTN = N_HEADS * V_DIM
Q_BLOCK = 128
NUM_BUCKETS = 32
MAX_EXACT = NUM_BUCKETS // 2
MAX_DISTANCE = 128
D_FF = ((int(math.ceil(8 * D_MODEL / 3)) + 255) // 256) * 256


def _layernorm(x, g, b):
    xf = x.astype(jnp.float32)
    mu = jnp.mean(xf, axis=-1, keepdims=True)
    var = jnp.mean(jnp.square(xf - mu), axis=-1, keepdims=True)
    y = (xf - mu) * lax.rsqrt(var + LN_EPS)
    return (y * g.astype(jnp.float32) + b.astype(jnp.float32)).astype(x.dtype)

def _multiscale_pool(x, w, scale):
    B, S, D = x.shape
    xg = x.astype(jnp.float32).reshape(B, S, N_GROUPS, GROUP_W)
    cs = jnp.pad(jnp.cumsum(xg, axis=1), ((0, 0), (1, 0), (0, 0), (0, 0)))
    t = jnp.arange(S)
    pooled = []
    for g, win in enumerate(POOL_WINDOWS):
        hi = cs[:, 1:, g]
        lo = jnp.pad(cs[:, :S + 1 - win, g], ((0, 0), (win - 1, 0), (0, 0)))
        cnt = jnp.minimum(t + 1, win).astype(jnp.float32)[None, :, None]
        pooled.append((hi - lo) / cnt)
    pooled = jnp.stack(pooled, axis=2)
    mixed = jnp.einsum('bsgc,gcd->bsgd', pooled - xg, w.astype(jnp.float32))
    return (mixed.reshape(B, S, D) * scale.astype(jnp.float32)).astype(x.dtype)

def _rel_bucket(rel):
    n = jnp.maximum(rel, 0)
    is_small = n < MAX_EXACT
    nf = jnp.maximum(n, 1).astype(jnp.float32)
    large = MAX_EXACT + (jnp.log(nf / MAX_EXACT) / math.log(MAX_DISTANCE / MAX_EXACT)
                         * (NUM_BUCKETS - MAX_EXACT)).astype(jnp.int32)
    large = jnp.minimum(large, NUM_BUCKETS - 1)
    return jnp.where(is_small, n, large)

def _diff_attention(x, w_qkv, w_o, lam_p, subln_g, rel_table, lambda_init):
    B, S, D = x.shape
    qkv = x @ w_qkv
    q, k, v = jnp.split(qkv, 3, axis=-1)
    q = q.reshape(B, S, N_HEADS, 2, HEAD_DIM).transpose(0, 2, 3, 1, 4)
    k = k.reshape(B, S, N_HEADS, 2, HEAD_DIM).transpose(0, 2, 3, 1, 4)
    v = v.reshape(B, S, N_HEADS, V_DIM).transpose(0, 2, 1, 3)
    lp = lam_p.astype(jnp.float32)
    lam = (jnp.exp(jnp.sum(lp[0] * lp[1])) - jnp.exp(jnp.sum(lp[2] * lp[3])) + lambda_init)
    sm_scale = HEAD_DIM ** -0.5
    outs = []
    for qb in range(S // Q_BLOCK):
        q0 = qb * Q_BLOCK
        kend = q0 + Q_BLOCK
        s = jnp.einsum('bhcqd,bhckd->bhcqk', q[:, :, :, q0:kend], k[:, :, :, :kend]).astype(jnp.float32) * sm_scale
        rel = (q0 + jnp.arange(Q_BLOCK))[:, None] - jnp.arange(kend)[None, :]
        bias = rel_table[_rel_bucket(rel)].astype(jnp.float32).transpose(2, 0, 1)
        s = jnp.where(rel >= 0, s + bias[None, :, None], -jnp.inf)
        p = jax.nn.softmax(s, axis=-1)
        a = p[:, :, 0] - lam * p[:, :, 1]
        outs.append(jnp.einsum('bhqk,bhkv->bhqv', a.astype(v.dtype), v[:, :, :kend]))
    o = jnp.concatenate(outs, axis=2).astype(jnp.float32)
    o = o * lax.rsqrt(jnp.mean(jnp.square(o), axis=-1, keepdims=True) + LN_EPS)
    o = o * subln_g.astype(jnp.float32) * (1.0 - lambda_init)
    o = o.transpose(0, 2, 1, 3).reshape(B, S, D_ATTN).astype(x.dtype)
    return o @ w_o

def _swiglu(x, w_gate, w_up, w_down):
    return (jax.nn.silu(x @ w_gate) * (x @ w_up)) @ w_down

def first_inputs(seed: int = 0) -> dict:
    key = jax.random.key(seed)
    ks = jax.random.split(key, 20)
    f32 = jnp.float32
    nrm = lambda k, s: jax.random.normal(k, s, f32)
    x = nrm(ks[0], (BATCH, SEQ, D_MODEL))
    pool_w = nrm(ks[1], (N_POOL_LAYERS, N_GROUPS, GROUP_W, GROUP_W)) * (GROUP_W ** -0.5) * BETA
    pool_scale = 1.0 + 0.02 * nrm(ks[2], (N_POOL_LAYERS, D_MODEL))
    w_qk = nrm(ks[3], (N_ATTN_LAYERS, D_MODEL, 2 * D_ATTN)) * (D_MODEL ** -0.5)
    w_v = nrm(ks[4], (N_ATTN_LAYERS, D_MODEL, D_ATTN)) * (D_MODEL ** -0.5) * BETA
    w_qkv = jnp.concatenate([w_qk, w_v], axis=-1)
    w_o = nrm(ks[5], (N_ATTN_LAYERS, D_ATTN, D_MODEL)) * (D_ATTN ** -0.5) * BETA
    lam_p = 0.1 * nrm(ks[6], (N_ATTN_LAYERS, 4, HEAD_DIM))
    subln_g = 1.0 + 0.02 * nrm(ks[7], (N_ATTN_LAYERS, V_DIM))
    rel_table = 0.5 * nrm(ks[8], (NUM_BUCKETS, N_HEADS))
    w_gate = nrm(ks[9], (DEPTH, D_MODEL, D_FF)) * (D_MODEL ** -0.5) * BETA
    w_up = nrm(ks[10], (DEPTH, D_MODEL, D_FF)) * (D_MODEL ** -0.5) * BETA
    w_down = nrm(ks[11], (DEPTH, D_FF, D_MODEL)) * (D_FF ** -0.5) * BETA
    ln_mix_g = 1.0 + 0.02 * nrm(ks[12], (DEPTH, D_MODEL))
    ln_mix_b = 0.02 * nrm(ks[13], (DEPTH, D_MODEL))
    ln_ffn_g = 1.0 + 0.02 * nrm(ks[14], (DEPTH, D_MODEL))
    ln_ffn_b = 0.02 * nrm(ks[15], (DEPTH, D_MODEL))
    return {"x": x, "pool_w": pool_w, "pool_scale": pool_scale, "w_qkv": w_qkv, "w_o": w_o,
            "lam_p": lam_p, "subln_g": subln_g, "rel_table": rel_table, "w_gate": w_gate,
            "w_up": w_up, "w_down": w_down, "ln_mix_g": ln_mix_g, "ln_mix_b": ln_mix_b,
            "ln_ffn_g": ln_ffn_g, "ln_ffn_b": ln_ffn_b}

def first_block(x, pool_w, pool_scale, w_qkv, w_o, lam_p, subln_g, rel_table, w_gate,
              w_up, w_down, ln_mix_g, ln_mix_b, ln_ffn_g, ln_ffn_b):
    for i in range(DEPTH):
        j = i // N_MIXERS
        if i % N_MIXERS == 0:
            h = _multiscale_pool(x, pool_w[j], pool_scale[j])
        else:
            lambda_init = 0.8 - 0.6 * math.exp(-0.3 * i)
            h = _diff_attention(x, w_qkv[j], w_o[j], lam_p[j], subln_g[j], rel_table, lambda_init)
        x = _layernorm(ALPHA * x + h, ln_mix_g[i], ln_mix_b[i])
        x = _layernorm(ALPHA * x + _swiglu(x, w_gate[i], w_up[i], w_down[i]), ln_ffn_g[i], ln_ffn_b[i])
    return x


DEPTH_2 = 1

N_HEADS_A = 8
N_HEADS_B = 8
D_A = N_HEADS_A * HEAD_DIM
D_B = N_HEADS_B * HEAD_DIM
N_IDX_HEADS = 8
IDX_DIM = 64
D_RNN = 512
N_RNN_BLOCKS = 8
RNN_BLOCK = D_RNN // N_RNN_BLOCKS
CONV_WIDTH = 4
LRU_C = 8.0
D_FF_2 = 4 * D_MODEL
MOBA_BLOCK = 256
MOBA_TOPK = 3
DSA_MAX_TOPK = 256
N_BUCKETS = 32
N_BRANCHES = 3
N_ATTN_HEADS = N_HEADS_A + N_HEADS_B
EPS = 1e-6
NEG = -1e30

IN_SPLITS = (D_A, D_A, D_A,
             D_B, D_B, D_B,
             N_IDX_HEADS * IDX_DIM,
             IDX_DIM,
             N_IDX_HEADS,
             D_RNN, D_RNN,
             N_BRANCHES * D_MODEL)
D_IN = sum(IN_SPLITS)
IN_OFFSETS = tuple(int(o) for o in np.cumsum(IN_SPLITS)[:-1])


def rms_norm(x, g):
    xf = x.astype(jnp.float32)
    y = xf * lax.rsqrt(jnp.mean(xf * xf, axis=-1, keepdims=True) + EPS)
    return (y * g.astype(jnp.float32)).astype(x.dtype)

def t5_bucket(dist):
    n = jnp.maximum(dist, 0)
    max_exact = N_BUCKETS // 2
    nf = jnp.maximum(n, 1).astype(jnp.float32)
    large = max_exact + (jnp.log(nf / max_exact) / math.log(MAX_DISTANCE / max_exact)
                         * (N_BUCKETS - max_exact)).astype(jnp.int32)
    large = jnp.minimum(large, N_BUCKETS - 1)
    return jnp.where(n < max_exact, n, large)

def moba_attention(q, k, v, bias_tab):
    B, S, H, dh = q.shape
    nb = -(-S // MOBA_BLOCK)
    pad = nb * MOBA_BLOCK - S
    kp = jnp.pad(k, ((0, 0), (0, pad), (0, 0), (0, 0)))
    vp = jnp.pad(v, ((0, 0), (0, pad), (0, 0), (0, 0)))
    kblk = kp.reshape(B, nb, MOBA_BLOCK, H, dh).transpose(0, 3, 1, 2, 4)
    vblk = vp.reshape(B, nb, MOBA_BLOCK, H, dh).transpose(0, 3, 1, 2, 4)
    kmean = jnp.mean(kblk, axis=3)
    n_sel = min(MOBA_TOPK, nb)
    scale = dh ** -0.5
    b_ix = jnp.arange(B)[:, None, None, None]
    h_ix = jnp.arange(H)[None, None, :, None]
    blk_ids = jnp.arange(nb)
    bias_t = bias_tab.T

    def one_block(qb):
        t0 = qb * Q_BLOCK
        cur = t0 // MOBA_BLOCK
        t = t0 + jnp.arange(Q_BLOCK)
        qq = lax.dynamic_slice_in_dim(q, t0, Q_BLOCK, axis=1)
        gate = jnp.einsum('bqhd,bhnd->bqhn', qq, kmean).astype(jnp.float32)
        gate = jnp.where(blk_ids < cur, gate, NEG)
        _, sel = lax.top_k(gate, n_sel)
        sel_ok = sel < cur
        kg = kblk[b_ix, h_ix, sel]
        vg = vblk[b_ix, h_ix, sel]
        s_past = jnp.einsum('bqhd,bqhnkd->bqhnk', qq, kg).astype(jnp.float32) * scale
        pos_past = sel[..., None] * MOBA_BLOCK + jnp.arange(MOBA_BLOCK)
        bias_past = bias_t[h_ix[..., None], t5_bucket(t[None, :, None, None, None] - pos_past)]
        s_past = jnp.where(sel_ok[..., None], s_past + bias_past, NEG)
        k_own = lax.dynamic_slice_in_dim(kp, cur * MOBA_BLOCK, MOBA_BLOCK, axis=1)
        v_own = lax.dynamic_slice_in_dim(vp, cur * MOBA_BLOCK, MOBA_BLOCK, axis=1)
        rel = t[:, None] - (cur * MOBA_BLOCK + jnp.arange(MOBA_BLOCK))[None, :]
        bias_own = bias_tab[t5_bucket(rel)].transpose(0, 2, 1)[None]
        s_own = jnp.einsum('bqhd,bkhd->bqhk', qq, k_own).astype(jnp.float32) * scale + bias_own
        s_own = jnp.where((rel >= 0)[None, :, None, :], s_own, NEG)
        logits = jnp.concatenate([s_past.reshape(B, Q_BLOCK, H, n_sel * MOBA_BLOCK), s_own], axis=-1)
        p = jax.nn.softmax(logits, axis=-1).astype(v.dtype)
        p_past = p[..., :n_sel * MOBA_BLOCK].reshape(B, Q_BLOCK, H, n_sel, MOBA_BLOCK)
        p_own = p[..., n_sel * MOBA_BLOCK:]
        return (jnp.einsum('bqhnk,bqhnkd->bqhd', p_past, vg)
                + jnp.einsum('bqhk,bkhd->bqhd', p_own, v_own))

    out = lax.map(one_block, jnp.arange(S // Q_BLOCK))
    return out.transpose(1, 0, 2, 3, 4).reshape(B, S, H * dh)

def dsa_attention(q, k, v, qi, ki, wi, bias_tab):
    B, S, H, dh = q.shape
    n_keep = min(DSA_MAX_TOPK, S // 4)
    scale = dh ** -0.5
    idx_scale = (N_IDX_HEADS ** -0.5) * (IDX_DIM ** -0.5)
    s_all = jnp.arange(S)

    def one_block(qb):
        t0 = qb * Q_BLOCK
        t = t0 + jnp.arange(Q_BLOCK)
        qq = lax.dynamic_slice_in_dim(q, t0, Q_BLOCK, axis=1)
        qiq = lax.dynamic_slice_in_dim(qi, t0, Q_BLOCK, axis=1)
        wq = lax.dynamic_slice_in_dim(wi, t0, Q_BLOCK, axis=1)
        dots = jnp.einsum('bqhd,bsd->bqhs', qiq, ki)
        score = jnp.einsum('bqh,bqhs->bqs', wq, jax.nn.relu(dots)).astype(jnp.float32) * idx_scale
        score = jnp.where((s_all[None, :] <= t[:, None])[None], score, NEG)
        _, idx = lax.top_k(score, n_keep)
        ok = idx <= t[None, :, None]
        kg = jax.vmap(lambda kk, ii: kk[ii])(k, idx)
        vg = jax.vmap(lambda vv, ii: vv[ii])(v, idx)
        bias = bias_tab[t5_bucket(t[None, :, None] - idx)].transpose(0, 1, 3, 2)
        logits = jnp.einsum('bqhd,bqkhd->bqhk', qq, kg).astype(jnp.float32) * scale + bias
        logits = jnp.where(ok[:, :, None, :], logits, NEG)
        p = jax.nn.softmax(logits, axis=-1).astype(v.dtype)
        return jnp.einsum('bqhk,bqkhd->bqhd', p, vg)

    out = lax.map(one_block, jnp.arange(S // Q_BLOCK))
    return out.transpose(1, 0, 2, 3, 4).reshape(B, S, H * dh)

def causal_depthwise_conv(x, w, b):
    S = x.shape[1]
    xp = jnp.pad(x, ((0, 0), (CONV_WIDTH - 1, 0), (0, 0)))
    y = b
    for i in range(CONV_WIDTH):
        y = y + w[i] * xp[:, i:i + S]
    return y

def rg_lru(x, w_r, b_r, w_i, b_i, lam):
    B, S, C = x.shape
    xb = x.reshape(B, S, N_RNN_BLOCKS, RNN_BLOCK)
    r = jax.nn.sigmoid(jnp.einsum('bsnc,ncd->bsnd', xb, w_r).reshape(B, S, C) + b_r)
    i = jax.nn.sigmoid(jnp.einsum('bsnc,ncd->bsnd', xb, w_i).reshape(B, S, C) + b_i)
    log_a = -LRU_C * r.astype(jnp.float32) * jax.nn.softplus(-lam.astype(jnp.float32))
    a = jnp.exp(log_a)
    u = jnp.sqrt(-jnp.expm1(2.0 * log_a)) * (i * x).astype(jnp.float32)

    def combine(left, right):
        a1, b1 = left
        a2, b2 = right
        return a1 * a2, a2 * b1 + b2

    _, h = lax.associative_scan(combine, (a, u), axis=1)
    return h.astype(x.dtype)

def token_mixer(xn, w_in, conv_w, conv_b, w_r, b_r, w_i, b_i, lam, w_pa, w_pb, w_pc, w_o, rel_bias):
    B, S, _ = xn.shape
    proj = xn @ w_in
    (qa, ka, va, qb, kb, vb, qi, ki, wi, xc, yc, gates) = jnp.split(proj, IN_OFFSETS, axis=-1)
    heads_a = lambda z: z.reshape(B, S, N_HEADS_A, HEAD_DIM)
    heads_b = lambda z: z.reshape(B, S, N_HEADS_B, HEAD_DIM)
    y_a = moba_attention(heads_a(qa), heads_a(ka), heads_a(va), rel_bias[:, :N_HEADS_A])
    y_b = dsa_attention(heads_b(qb), heads_b(kb), heads_b(vb),
                        qi.reshape(B, S, N_IDX_HEADS, IDX_DIM), ki, wi, rel_bias[:, N_HEADS_A:])
    y_c = rg_lru(causal_depthwise_conv(xc, conv_w, conv_b), w_r, b_r, w_i, b_i, lam) * jax.nn.gelu(yc)
    g = jax.nn.sigmoid(gates).reshape(B, S, N_BRANCHES, D_MODEL)
    merged = g[:, :, 0] * (y_a @ w_pa) + g[:, :, 1] * (y_b @ w_pb) + g[:, :, 2] * (y_c @ w_pc)
    return merged @ w_o

def squared_relu_mlp(xn, w_up, w_down):
    return jnp.square(jax.nn.relu(xn @ w_up)) @ w_down

def second_inputs(seed: int = 0) -> dict:
    key = jax.random.key(seed)
    ks = jax.random.split(key, 20)
    f32 = jnp.float32
    nrm = lambda k, shape, s: jax.random.normal(k, shape, f32) * s
    u = jax.random.uniform(ks[10], (DEPTH_2, D_RNN), f32, minval=0.9, maxval=0.999)
    a = u ** (1.0 / LRU_C)
    lam = jnp.log(a) - jnp.log1p(-a)
    return {
        "x": nrm(ks[0], (BATCH, SEQ, D_MODEL), 1.0),
        "rel_bias": nrm(ks[1], (N_BUCKETS, N_ATTN_HEADS), 0.5),
        "norm_mix_g": 1.0 + nrm(ks[2], (DEPTH_2, D_MODEL), 0.05),
        "w_in": nrm(ks[3], (DEPTH_2, D_MODEL, D_IN), D_MODEL ** -0.5),
        "conv_w": nrm(ks[4], (DEPTH_2, CONV_WIDTH, D_RNN), CONV_WIDTH ** -0.5),
        "conv_b": nrm(ks[5], (DEPTH_2, D_RNN), 0.02),
        "w_r": nrm(ks[6], (DEPTH_2, N_RNN_BLOCKS, RNN_BLOCK, RNN_BLOCK), RNN_BLOCK ** -0.5),
        "b_r": nrm(ks[7], (DEPTH_2, D_RNN), 0.1),
        "w_i": nrm(ks[8], (DEPTH_2, N_RNN_BLOCKS, RNN_BLOCK, RNN_BLOCK), RNN_BLOCK ** -0.5),
        "b_i": nrm(ks[9], (DEPTH_2, D_RNN), 0.1),
        "lru_lambda": lam,
        "w_pa": nrm(ks[11], (DEPTH_2, D_A, D_MODEL), D_A ** -0.5),
        "w_pb": nrm(ks[12], (DEPTH_2, D_B, D_MODEL), D_B ** -0.5),
        "w_pc": nrm(ks[13], (DEPTH_2, D_RNN, D_MODEL), D_RNN ** -0.5),
        "w_o": nrm(ks[14], (DEPTH_2, D_MODEL, D_MODEL), D_MODEL ** -0.5),
        "norm_mlp_g": 1.0 + nrm(ks[15], (DEPTH_2, D_MODEL), 0.05),
        "w_up": nrm(ks[16], (DEPTH_2, D_MODEL, D_FF_2), D_MODEL ** -0.5),
        "w_down": nrm(ks[17], (DEPTH_2, D_FF_2, D_MODEL), D_FF_2 ** -0.5),
        "final_norm_g": 1.0 + nrm(ks[18], (D_MODEL,), 0.05),
    }

def second_block(x, rel_bias, norm_mix_g, w_in, conv_w, conv_b, w_r, b_r, w_i, b_i, lru_lambda,
              w_pa, w_pb, w_pc, w_o, norm_mlp_g, w_up, w_down, final_norm_g):
    for l in range(DEPTH_2):
        x = x + token_mixer(rms_norm(x, norm_mix_g[l]), w_in[l], conv_w[l], conv_b[l],
                            w_r[l], b_r[l], w_i[l], b_i[l], lru_lambda[l],
                            w_pa[l], w_pb[l], w_pc[l], w_o[l], rel_bias)
        x = x + squared_relu_mlp(rms_norm(x, norm_mlp_g[l]), w_up[l], w_down[l])
    return rms_norm(x, final_norm_g)


def setup_inputs(seed=0):
    out = dict(first_inputs(seed))
    for name, value in second_inputs(seed + 1).items():
        if name != "x":
            out[name + "_2"] = value
    return out


def reference(
    x, pool_w, pool_scale, w_qkv, w_o, lam_p, subln_g, rel_table, w_gate, w_up, w_down,
    ln_mix_g, ln_mix_b, ln_ffn_g, ln_ffn_b, rel_bias_2, norm_mix_g_2, w_in_2, conv_w_2,
    conv_b_2, w_r_2, b_r_2, w_i_2, b_i_2, lru_lambda_2, w_pa_2, w_pb_2, w_pc_2, w_o_2,
    norm_mlp_g_2, w_up_2, w_down_2, final_norm_g_2,
):
    x = first_block(
        x, pool_w, pool_scale, w_qkv, w_o, lam_p, subln_g, rel_table, w_gate, w_up, w_down,
        ln_mix_g, ln_mix_b, ln_ffn_g, ln_ffn_b,
    )
    return second_block(
        x, rel_bias_2, norm_mix_g_2, w_in_2, conv_w_2, conv_b_2, w_r_2, b_r_2, w_i_2, b_i_2,
        lru_lambda_2, w_pa_2, w_pb_2, w_pc_2, w_o_2, norm_mlp_g_2, w_up_2, w_down_2,
        final_norm_g_2,
    )


_drawn_inputs = setup_inputs


def setup_inputs(seed=0):
    import zlib

    import numpy as np

    out = dict(_drawn_inputs(seed))
    spreads = {}
    factors = {'pool_scale': 4.373, 'subln_g': 5.042, 'b_r_2': 8.0, 'b_i_2': 6.576}
    for name, (base, spread) in spreads.items():
        noise = np.random.default_rng([zlib.crc32(name.encode()), seed]).standard_normal(out[name].shape)
        drawn = base * np.exp(spread * noise) if base else spread * noise
        out[name] = __import__('jax').numpy.asarray(drawn.astype(out[name].dtype))
    for name, factor in factors.items():
        out[name] = (out[name] * factor).astype(out[name].dtype)
    return out
```

```python
import math
from contextlib import ExitStack

import numpy as np

import concourse.bass as bass
from concourse import mybir

F32 = mybir.dt.float32
F32R = mybir.dt.float32r
ALU = mybir.AluOpType
ACT = mybir.ActivationFunctionType

P = 128
SEQ = 256
NT = SEQ // P
D = 1024
KT = D // P
DFF = 2816
DFF2 = 4096
DEPTH = 2
ALPHA = (2.0 * DEPTH) ** 0.25
LN_EPS = 1e-5
EPS = 1e-6
WINDOWS = (2, 4, 8, 16)
NG = len(WINDOWS)
HEADS = 8
DH = 64
VD = 128
LAMBDA_INIT = 0.8 - 0.6 * math.exp(-0.3)
NBUCK = 32
MAXD = 128
D_RNN = 512
CT = D_RNN // P
LRU_C = 8.0
TOPK = SEQ // 4
IDX_HEADS = 8
IDX_SCALE = IDX_HEADS ** -0.5 * DH ** -0.5
SM = DH ** -0.5
NEG = -1e30
TAKEN = -3e38
ROOT_MIN = 2.0 ** -116
GELU_A = 0.044715
GELU_B = 2.0 * math.sqrt(2.0 / math.pi)

(O_QA, O_KA, O_VA, O_QB, O_KB, O_VB, O_QI, O_KI, O_WI, O_XC, O_YC, O_GT) = (
    0, 512, 1024, 1536, 2048, 2560, 3072, 3584, 3648, 3656, 4168, 4680)
D_IN = 7752

UW = 2048
SLOTS = 3
CH = 256
NCH = DFF // CH
NCH2 = DFF2 // CH
U_FFN = [0, 0]
U_FFN[0] = 0
U_V = U_FFN[0] + 3 * NCH
U_HEAD = U_V + 4
U_WO = U_HEAD + HEADS
U_FFN[1] = U_WO + 4
U_QI = U_FFN[1] + 3 * NCH
U_KI = U_QI + 2
U_VA = U_KI + 1
U_VB = U_VA + 2
U_MOBA = U_VB + 2
U_XC = U_MOBA + 4
U_DSA = U_XC + 2
U_YC = U_DSA + 4
U_GATE = U_YC + 2
U_WO2 = U_GATE + 18
U_MLP = U_WO2 + 4
U_END = U_MLP + 2 * NCH2

A_MOBA, A_DSA, A_END = 8, 12, 16


def step_of(unit):
    if U_HEAD <= unit < U_HEAD + 8:
        return unit - U_HEAD
    if U_MOBA <= unit < U_MOBA + 4:
        return A_MOBA + unit - U_MOBA
    if U_DSA <= unit < U_DSA + 4:
        return A_DSA + unit - U_DSA
    return None


def mixer_turns():
    turns = []
    started, scored, applied = A_MOBA, A_MOBA, A_MOBA
    for unit in range(U_QI, U_GATE):
        apply = applied if applied < scored else None
        score = scored if scored < started else None
        applied += apply is not None
        scored += score is not None
        started += step_of(unit) is not None
        turns.append((unit, apply, score))
    assert applied == scored == started == A_END
    return turns


TURNS = mixer_turns()
HEAD_TURNS = [(U_HEAD + i if i < 8 else None, i - 2 if i >= 2 else None, i - 1 if 1 <= i <= 8 else None)
              for i in range(10)]

COPIED = {}
for _u in (*range(U_HEAD, U_HEAD + 8), *range(U_QI, U_KI + 1), *range(U_MOBA, U_GATE)):
    COPIED[_u] = len(COPIED)

ROWS = {}
_row = 0
for _name, _n in (("ln_mix_g", 16), ("ln_mix_b", 16), ("ln_ffn_g", 16), ("ln_ffn_b", 16), ("norm_mix_g_2", 8),
                  ("norm_mlp_g_2", 8), ("conv_b_2", 4), ("b_r_2", 4), ("b_i_2", 4), ("lru_lambda_2", 4),
                  ("conv_w_2", 16), ("subln_g", 1)):
    ROWS[_name] = (_row, _n)
    _row += _n
NROWS = _row


def buckets():
    rel = 255 - np.arange(384)
    n = np.maximum(rel, 0)
    nf = np.maximum(n, 1).astype(np.float32)
    large = 16 + (np.log(nf / np.float32(16)) / np.float32(math.log(MAXD / 16)) * np.float32(16)).astype(np.int32)
    b = np.where(n < 16, n, np.minimum(large, NBUCK - 1))
    one = ((b[None] == np.arange(NBUCK)[:, None]) & (rel >= 0)[None]).astype(np.float32)
    mask = np.broadcast_to(np.where(rel >= 0, 0.0, NEG / SM).astype(np.float32), (24, 384))
    return one, np.ascontiguousarray(mask)


def pool_matrices():
    m = np.zeros((P, NG, 384), np.float32)
    for g, w in enumerate(WINDOWS):
        full = np.zeros((SEQ, SEQ), np.float32)
        for t in range(SEQ):
            full[max(0, t + 1 - w):t + 1, t] = np.float32(1.0) / np.float32(min(t + 1, w))
        full -= np.eye(SEQ, dtype=np.float32)
        m[:, g, 0:256] = full[0:128, :]
        m[:, g, 256:384] = full[128:, 128:]
    return m


def constants():
    one, mask = buckets()
    causal = np.zeros((P, 256), np.float32)
    causal[:, 128:] = np.triu(np.full((P, P), NEG, np.float32), 1)
    return {"c_onehot": one, "c_vecmask": mask, "c_pool": pool_matrices(), "c_causal": causal,
            "c_ident": np.eye(P, dtype=np.float32)}


def build(nc, t, out):
    with ExitStack() as ctx:
        def sb(name, shape, dt=F32):
            return ctx.enter_context(nc.sbuf_tensor(name, shape, dt))

        def sem(name):
            return ctx.enter_context(nc.semaphore(name))

        raw = [sb(f"raw{s}", [P, UW]) for s in range(SLOTS)]
        w_hi = [sb(f"w_hi{s}", [P, UW], F32R) for s in range(SLOTS)]
        w_lo = [sb(f"w_lo{s}", [P, UW], F32R) for s in range(SLOTS)]
        x = sb("x_rows", [P, NT, D])
        x_hi = sb("x_hi", [P, KT, SEQ], F32R)
        x_lo = sb("x_lo", [P, KT, SEQ], F32R)
        table = sb("table", [P, 16, SEQ])
        gb = sb("gb", [P, 2, D])
        ident = sb("ident", [P, P])
        causal = sb("causal", [P, SEQ])
        par = sb("par", [P, NROWS])
        neg_b = sb("neg_b", [P, 8])
        lru_c = sb("lru_c", [P, CT])
        sp = sb("sp", [P, 4, CT])
        neg_lam = sb("neg_lam", [P, 1])
        e_lam = sb("e_lam", [P, 2])
        sub_gain = sb("sub_gain", [P, 1])
        wi_s = sb("wi_s", [P, NT, IDX_HEADS])
        stats = sb("stats", [P, NT, 2, 6])
        mv = sb("mv", [P, NT, 2])
        vareps = sb("vareps", [P, 16])
        rstd = sb("rstd", [P, 16])
        minus_half = sb("minus_half", [P, 1])
        nmax = sb("nmax", [P, 2, 2])
        zsum = sb("zsum", [P, 2, 2])
        rz = sb("rz", [P, 2, 2])
        sumsq = sb("sumsq", [P, 2, HEADS])
        top8 = sb("top8", [P, 2, 8])
        arena = sb("arena", [P, 13728])
        arena_r = sb("arena_r", [P, 6144], F32R)

        def view(at, *dims):
            n = int(np.prod(dims))
            v = arena[:, at:at + n]
            if len(dims) == 2:
                v = v.rearrange("p (a b) -> p a b", a=dims[0])
            if len(dims) == 3:
                v = v.rearrange("p (a b c) -> p a b c", a=dims[0], b=dims[1])
            return v

        ffn_e, ffn_t, ffn_h = view(0, 512), view(512, 512), view(1024, 512)
        h_hi = arena_r[:, 0:512].rearrange("p (a b) -> p a b", a=2)
        h_lo = arena_r[:, 512:1024].rearrange("p (a b) -> p a b", a=2)
        pool_m, pool_w, pool_d = view(0, NG, 384), view(2048, NG, 2, 256), view(4096, KT, SEQ)
        onehot, vecmask, vec, tab = (arena[0:32, 12288:12672], arena[0:24, 12672:13056], arena[0:24, 13056:13440],
                                     arena[0:32, 13440:13464])
        lp, lprod, ones = arena[0:64, 13464:13468], arena[0:64, 13468:13470], arena[0:64, 13472:13600]
        prow = arena[0:NROWS, 13600:13728]
        xf, nbuf = view(8192, KT, SEQ), view(10240, NT, D)
        v1, o1 = view(0, NT, D), view(2048, NT, D)
        qk = [view(4096 + 512 * i, 2, SEQ) for i in range(2)]
        logit, prob_e, prob, prob_t = view(5120, 2, 384), view(5888, 2, 384), view(6656, 2, 384), view(7424, 2, 384)
        v_a, v_b = view(0, NT, 512), view(1024, NT, 512)
        qi, ki, dots = view(2048, 4, SEQ), view(3072, SEQ), view(3328, 2, 384)
        score, work, chosen = view(8192, 384), view(8576, 384), view(8960, 384)
        y_hi = arena_r[:, 0:3072].rearrange("p (b k n) -> p b k n", b=3, k=4)
        y_lo = arena_r[:, 3072:6144].rearrange("p (b k n) -> p b k n", b=3, k=4)
        xc, conv, yc, wri = view(9344, CT, 260), view(10384, CT, SEQ), view(11408, CT, SEQ), view(12432, 2, CT, P)
        gr, gi, ra, rt = (view(4096 + 1024 * i, CT, SEQ) for i in range(4))
        rq, gl = view(12432, CT, SEQ), view(8192, CT, SEQ)
        head_scr, sq_scr = view(8192, NT, P), view(8192, NT, D)
        merged, sig, prod = view(0, KT, SEQ), view(2048, 4, SEQ), view(3072, 4, SEQ)

        bank = [ctx.enter_context(nc.psum_tensor(f"bank{i}", [P, 512], F32)) for i in range(8)]
        vec_dram = nc.dram_tensor("bias_vectors", (24, P, 384), F32, kind="Internal").ap()

        raw_in = [sem(f"raw_in{s}") for s in range(SLOTS)]
        hi_done = sem("hi_done")
        lo_done = sem("lo_done")
        unit_done = sem("unit_done")
        gate_read = sem("gate_read")
        up_read = sem("up_read")
        sig_step = sem("sig_step")
        exp_done = sem("exp_done")
        h_rounded = sem("h_rounded")
        h_ready = sem("h_ready")
        relu_done = sem("relu_done")
        sq_done = sem("sq_done")
        m_rounded = sem("m_rounded")
        m_ready = sem("m_ready")
        x_in = sem("x_in")
        small_in = sem("small_in")
        pool_in = sem("pool_in")
        vec_out = sem("vec_out")
        table_in = sem("table_in")
        table2_in = sem("table2_in")
        gb_in = sem("gb_in")
        gb_used = sem("gb_used")
        wri_in = sem("wri_in")
        set_done = sem("set_done")
        wri_zero = sem("wri_zero")
        pe_start = sem("pe_start")
        v_start = sem("v_start")
        s_start = sem("s_start")
        pooled = sem("pooled")
        pool_copied = sem("pool_copied")
        mixed = sem("mixed")
        v_link = sem("v_link")
        s_link = sem("s_link")
        var_ready = sem("var_ready")
        rstd_ready = sem("rstd_ready")
        ss_ready = sem("ss_ready")
        z_ready = sem("z_ready")
        n_ready = sem("n_ready")
        n_turned = sem("n_turned")
        xf_ready = sem("xf_ready")
        x_rounded = sem("x_rounded")
        x_ready = sem("x_ready")
        nat_ready = sem("nat_ready")
        nat_link = sem("nat_link")
        v_copied = sem("v_copied")
        proj_copied = sem("proj_copied")
        scored = sem("scored")
        logits_read = sem("logits_read")
        exp_ready = sem("exp_ready")
        prob_ready = sem("prob_ready")
        turned = sem("turned")
        pt_copied = sem("pt_copied")
        pt_copied2 = sem("pt_copied2")
        applied = sem("applied")
        o_copied = sem("o_copied")
        o_squared = sem("o_squared")
        dotted = sem("dotted")
        dots_relu = sem("dots_relu")
        dots_used = sem("dots_used")
        conv_ready = sem("conv_ready")
        ri_ready = sem("ri_ready")
        ri_exp = sem("ri_exp")
        ri_sig = sem("ri_sig")
        lru_act = sem("lru_act")
        lru_u2 = sem("lru_u2")
        lru_root = sem("lru_root")
        gelu_sq = sem("gelu_sq")
        gelu_z = sem("gelu_z")
        gelu_e = sem("gelu_e")
        yc_ready = sem("yc_ready")
        yc_rounded = sem("yc_rounded")
        y_ready = sem("y_ready")
        gate_exp = sem("gate_exp")
        p_read = sem("p_read")
        merged_ready = sem("merged_ready")
        out_ready = sem("out_ready")
        stored = sem("stored")

        block = ctx.enter_context(nc.Block())

        def col(name, k=0):
            at = ROWS[name][0] + k
            return par[:, at:at + 1]

        def part(tile, slot, a):
            return tile[slot][:, :].rearrange("p (a b) -> p a b", a=a)

        def by_rows(w, k0, nk, c0, nc_):
            return w[k0 * P:(k0 + nk) * P, c0:c0 + nc_].rearrange("(k p) c -> p k c", p=P)

        def load(eng, unit, slot, parts, waits=True):
            if waits:
                eng.wait_ge(lo_done, unit - (SLOTS - 1))
            for dst, src in parts:
                eng.dma_start(dst, src).then_inc(raw_in[slot], 16)

        def halved(slot, src):
            a, b = src.shape[1:]
            dst = raw[slot][:, 0:a * b].rearrange("p (a b) -> p a b", a=a)
            return [(dst[:, h * a // 2:(h + 1) * a // 2, :], src[:, h * a // 2:(h + 1) * a // 2, :]) for h in (0, 1)]

        def load_unit(eng, unit, src):
            load(eng, unit, unit % SLOTS, halved(unit % SLOTS, src), unit >= SLOTS)

        def load_heads(eng, unit, w, q0, k0):
            dst = part(raw, unit % SLOTS, KT)
            load(eng, unit, unit % SLOTS, [(dst[:, :, h * P:(h + 1) * P], by_rows(w, 0, KT, c, P))
                                           for h, c in enumerate((q0, k0))])

        def load_ffn(eng, f):
            u0 = U_FFN[f]
            gate, up, down = t["w_gate"][f], t["w_up"][f], t["w_down"][f]
            load_unit(eng, u0, by_rows(gate, 0, KT, 0, CH))
            load_unit(eng, u0 + 1, by_rows(up, 0, KT, 0, CH))
            first = 1
            if u0 == 0:
                load_unit(eng, 2, by_rows(gate, 0, KT, CH, CH))
                load_unit(eng, 3, by_rows(up, 0, KT, CH, CH))
                load_unit(eng, 4, by_rows(down, 0, 2, 0, D))
                first = 2
            slots = [(u0 + 2 + j) % SLOTS for j in range(3)]
            with eng.Fori(first, NCH) as i:
                unit = i * 3 + (u0 - 1)
                for j, w in ((0, gate), (1, up)):
                    load(eng, unit + j, slots[j],
                         halved(slots[j], w[:, bass.ds(i * CH, CH)].rearrange("(k p) c -> p k c", p=P)))
                load(eng, unit + 2, slots[2],
                     halved(slots[2], down[bass.ds(i * CH - CH, CH), :].rearrange("(k p) c -> p k c", p=P)))
            load_unit(eng, u0 + 3 * NCH - 1, by_rows(down, DFF // P - 2, 2, 0, D))

        def load_mlp(eng):
            up, down = t["w_up_2"], t["w_down_2"]
            load_unit(eng, U_MLP, by_rows(up, 0, KT, 0, CH))
            slots = [(U_MLP + 1 + j) % SLOTS for j in range(6)]
            with eng.Fori(0, (NCH2 - 1) // 3) as i:
                for j in range(3):
                    unit = i * 6 + (U_MLP + 1 + 2 * j)
                    load(eng, unit, slots[2 * j], halved(
                        slots[2 * j], up[:, bass.ds(i * (3 * CH) + (j + 1) * CH, CH)].rearrange(
                            "(k p) c -> p k c", p=P)))
                    load(eng, unit + 1, slots[2 * j + 1], halved(
                        slots[2 * j + 1], down[bass.ds(i * (3 * CH) + j * CH, CH), :].rearrange(
                            "(k p) c -> p k c", p=P)))
            load_unit(eng, U_END - 1, by_rows(down, DFF2 // P - 2, 2, 0, D))

        @block.sync
        def _(eng):
            eng.dma_start(x[:, :, :], t["x"].rearrange("(i p) d -> p i d", p=P)).then_inc(x_in, 16)
            eng.dma_start(pool_m, t["c_pool"]).then_inc(pool_in, 16)
            eng.dma_start(pool_w, t["pool_w"].rearrange("g (k p) d -> p g k d", p=P)).then_inc(pool_in, 16)
            load_ffn(eng, 0)
            w = t["w_qkv"]
            for j in range(4):
                load_unit(eng, U_V + j, by_rows(w, 2 * j, 2, 2 * D, D))
            for h in range(HEADS):
                load_heads(eng, U_HEAD + h, w, h * VD, D + h * VD)
            for j in range(4):
                load_unit(eng, U_WO + j, by_rows(t["w_o"], 2 * j, 2, 0, D))
            load_ffn(eng, 1)
            w = t["w_in_2"]
            for j in range(2):
                load_unit(eng, U_QI + j, by_rows(w, 0, KT, O_QI + 256 * j, 256))
            load_unit(eng, U_KI, by_rows(w, 0, KT, O_KI, 72))
            for j in range(2):
                load_unit(eng, U_VA + j, by_rows(w, 4 * j, 4, O_VA, 512))
            for j in range(2):
                load_unit(eng, U_VB + j, by_rows(w, 4 * j, 4, O_VB, 512))
            for j in range(4):
                load_heads(eng, U_MOBA + j, w, O_QA + P * j, O_KA + P * j)
            for j in range(2):
                load_unit(eng, U_XC + j, by_rows(w, 0, KT, O_XC + 256 * j, 256))
            for j in range(4):
                load_heads(eng, U_DSA + j, w, O_QB + P * j, O_KB + P * j)
            for j in range(2):
                load_unit(eng, U_YC + j, by_rows(w, 0, KT, O_YC + 256 * j, 256))
            for c in range(6):
                half, b = c // 3, c % 3
                for j in range(2):
                    load_unit(eng, U_GATE + 3 * c + j, by_rows(w, 0, KT, O_GT + b * D + half * 512 + j * 256, 256))
                load_unit(eng, U_GATE + 3 * c + 2,
                          by_rows(t[("w_pa_2", "w_pb_2", "w_pc_2")[b]], 0, 4, half * 512, 512))
            for j in range(4):
                load_unit(eng, U_WO2 + j, by_rows(t["w_o_2"], 2 * j, 2, 0, D))
            load_mlp(eng)
            for i in range(NT):
                eng.wait_ge(out_ready, i + 1)
                eng.dma_start(out[i * P:(i + 1) * P, :], x[:, i, :]).then_inc(stored, 16)
            eng.wait_ge(stored, 16 * NT)
            eng.wait_ge(vec_out, 16)

        def mm(*a, **k):
            return nc.tensor.matmul(*a, skip_group_check=True, **k)

        def three(out_, w, w_rest, a, a_rest, start, stop):
            mm(out_, w, a, start=start, stop=False)
            mm(out_, w, a_rest, start=False, stop=False)
            return mm(out_, w_rest, a, start=False, stop=stop)

        SMALL = 16 * (len(ROWS) + 7)

        def project(slot, outs, hi, lo, nk=KT):
            whi, wlo = (part(w, slot, nk) for w in (w_hi, w_lo))
            for j, o in enumerate(outs):
                for k in range(nk):
                    c = slice(j * P, (j + 1) * P)
                    last = three(o, whi[:, k, c], wlo[:, k, c], hi[:, k, :], lo[:, k, :], k == 0, k == nk - 1)
            return last

        def rows(slot, banks, hi, lo, k0, nk, width, first, final):
            whi, wlo = (part(w, slot, nk) for w in (w_hi, w_lo))
            for i in range(NT):
                for k in range(nk):
                    a, al = (v[:, k0 + k, i * P:(i + 1) * P] for v in (hi, lo))
                    start, stop = first and k == 0, final and k == nk - 1
                    cols = [slice(n * 512, (n + 1) * 512) for n in range(width // 512)]
                    for n, c in enumerate(cols):
                        mm(banks[i][n], a, whi[:, k, c], start=start, stop=False)
                    for n, c in enumerate(cols):
                        mm(banks[i][n], a, wlo[:, k, c], start=False, stop=False)
                    for n, c in enumerate(cols):
                        last = mm(banks[i][n], al, whi[:, k, c], start=False, stop=stop)
            return last

        acc = [[bank[0][:, :], bank[1][:, :]], [bank[2][:, :], bank[3][:, :]]]
        two4 = [bank[4][:, 0:256], bank[4][:, 256:512]]
        two5 = [bank[5][:, 0:256], bank[5][:, 256:512]]

        def pe_norm(eng, ev, src, ready):
            for i in range(NT):
                eng.wait_ge(n_ready, NT * ev + i + 1)
                for k in range(KT):
                    at = (k % 2) * 256 + i * P
                    last = nc.tensor.transpose(bank[4 + k // 2][:, at:at + P], src[:, i, k * P:(k + 1) * P],
                                               ident[:, :])
            last.then_inc(n_turned, 1)
            eng.wait_ge(x_ready, ready)

        def pe_ffn(eng, f):
            u0 = U_FFN[f]
            slots = [(u0 + 2 + j) % SLOTS for j in range(3)]

            def gate_up(i, unit):
                for j, banks in ((0, two4), (1, two5)):
                    eng.wait_ge(lo_done, unit + (j + 1))
                    eng.wait_ge((gate_read, up_read)[j], i + f * NCH)
                    project(slots[j], banks, x_hi, x_lo).then_inc(unit_done, 1)

            def down(i, unit, slot, first, final):
                eng.wait_ge(lo_done, unit + 1)
                eng.wait_ge(h_ready, i + (f * NCH + 1))
                rows(slot, acc, h_hi, h_lo, 0, 2, D, first, final).then_inc(unit_done, 1)

            eng.wait_ge(lo_done, u0 + 1)
            project(u0 % SLOTS, two4, x_hi, x_lo).then_inc(unit_done, 1)
            eng.wait_ge(lo_done, u0 + 2)
            project((u0 + 1) % SLOTS, two5, x_hi, x_lo).then_inc(unit_done, 1)
            gate_up(1, u0 + 2)
            down(0, u0 + 4, slots[2], True, False)
            with eng.Fori(2, NCH) as i:
                unit = i * 3 + (u0 - 1)
                gate_up(i, unit)
                down(i - 1, unit + 2, slots[2], False, False)
            down(NCH - 1, u0 + 3 * NCH - 1, (u0 + 3 * NCH - 1) % SLOTS, False, True)

        def pe_mlp(eng):
            def up(i, unit, slot):
                eng.wait_ge(lo_done, unit + 1)
                eng.wait_ge(sq_done, i)
                project(slot, two4, x_hi, x_lo).then_inc(unit_done, 1)

            def down(i, unit, slot, first, final):
                eng.wait_ge(lo_done, unit + 1)
                eng.wait_ge(m_ready, i + 1)
                rows(slot, acc, h_hi, h_lo, 0, 2, D, first, final).then_inc(unit_done, 1)

            eng.wait_ge(lo_done, U_MLP + 1)
            project(U_MLP % SLOTS, two4, x_hi, x_lo).then_inc(unit_done, 1)
            for j in range(3):
                unit = U_MLP + 1 + 2 * j
                up(j + 1, unit, unit % SLOTS)
                down(j, unit + 1, (unit + 1) % SLOTS, j == 0, False)
            with eng.Fori(1, (NCH2 - 1) // 3) as i:
                for j in range(3):
                    unit = i * 6 + (U_MLP + 1 + 2 * j)
                    up(i * 3 + (j + 1), unit, (U_MLP + 1 + 2 * j) % SLOTS)
                    down(i * 3 + j, unit + 1, (U_MLP + 2 + 2 * j) % SLOTS, False, False)
            down(NCH2 - 1, U_END - 1, (U_END - 1) % SLOTS, False, True)

        def pe_turn_probs(eng, a):
            eng.wait_ge(prob_ready, a + 1)
            if 1 <= a <= A_MOBA:
                eng.wait_ge(pt_copied, a)
            elif a > A_MOBA:
                eng.wait_ge(pt_copied2, a - A_MOBA)
            for m in range(1 if a < A_MOBA else 2):
                for b in range(3):
                    c = slice(b * P, (b + 1) * P)
                    last = nc.tensor.transpose(bank[6 + m][:, c], prob[:, m, c], ident[:, :])
            last.then_inc(turned, 1)

        def pe_score(eng, a, unit):
            eng.wait_ge(proj_copied, COPIED[unit] + 1)
            if a >= 2:
                eng.wait_ge(logits_read, a - 1)
            q_k = qk[a % 2]
            for m in range(2):
                s, r = bank[2 * (a % 2) + m], slice(m * DH, (m + 1) * DH)
                mm(s[:, 0:P], q_k[r, 0, 0:P], q_k[r, 1, 0:P], start=True, stop=True)
                last = mm(s[:, P:384], q_k[r, 0, P:SEQ], q_k[r, 1, 0:SEQ], start=True, stop=True)
            last.then_inc(scored, 1)

        def pe_apply(eng, a):
            if a < A_MOBA:
                eng.wait_ge(pt_copied, a + 1)
            else:
                eng.wait_ge(pt_copied2, a - A_MOBA + 1)
            if a >= 1:
                eng.wait_ge(o_copied, a)
            if a < A_MOBA:
                h = slice(a * VD, (a + 1) * VD)
                mm(bank[5][:, 0:P], prob_t[:, 0, 0:P], v1[:, 0, h], start=True, stop=True)
                mm(bank[5][:, P:SEQ], prob_t[:, 0, P:SEQ], v1[:, 0, h], start=True, stop=False)
                last = mm(bank[5][:, P:SEQ], prob_t[:, 0, SEQ:384], v1[:, 1, h], start=False, stop=True)
            else:
                v = v_a if a < A_DSA else v_b
                for m in range(2):
                    hd = 2 * ((a - A_MOBA) % 4) + m
                    o, h = bank[5][m * DH:(m + 1) * DH, :], slice(hd * DH, (hd + 1) * DH)
                    mm(o[:, 0:SEQ], v[:, 0, h], prob_t[:, m, 0:SEQ], start=True, stop=False)
                    last = mm(o[:, P:SEQ], v[:, 1, h], prob_t[:, m, SEQ:384], start=False, stop=True)
            last.then_inc(applied, 1)

        def pe_dots(eng, g):
            if g >= 1:
                eng.wait_ge(dots_relu, 2 * g)
            for m in range(2):
                r, s = slice(m * DH, (m + 1) * DH), bank[2 + m]
                mm(s[:, 0:P], qi[r, g, 0:P], ki[r, 0:P], start=True, stop=True)
                last = mm(s[:, P:384], qi[r, g, P:SEQ], ki[r, 0:SEQ], start=True, stop=True)
            last.then_inc(dotted, 1)

        def pe_mixer(eng):
            score_unit = {step_of(u): u for u in range(U_QI, U_GATE)}
            for unit, apply, score_step in TURNS:
                if apply is not None:
                    pe_turn_probs(eng, apply)
                if score_step is not None:
                    pe_score(eng, score_step, score_unit[score_step])
                eng.wait_ge(lo_done, unit + 1)
                s = unit % SLOTS
                if unit in COPIED:
                    eng.wait_ge(proj_copied, COPIED[unit])
                if unit == U_KI:
                    whi, wlo = (part(w, s, KT) for w in (w_hi, w_lo))
                    for k in range(KT):
                        three(bank[4][:, 0:SEQ], whi[:, k, 0:P], wlo[:, k, 0:P], x_hi[:, k, :], x_lo[:, k, :],
                              k == 0, k == KT - 1)
                    for i in range(NT):
                        c, tk = slice(P, P + IDX_HEADS), slice(i * P, (i + 1) * P)
                        for k in range(KT):
                            last = three(bank[4][:, 256 + 8 * i:264 + 8 * i], x_hi[:, k, tk], x_lo[:, k, tk],
                                         whi[:, k, c], wlo[:, k, c], k == 0, k == KT - 1)
                elif U_VA <= unit < U_MOBA:
                    j = (unit - U_VA) % 2
                    if unit == U_VB:
                        eng.wait_ge(v_copied, 2)
                    last = rows(s, [[bank[0][:, :]], [bank[1][:, :]]], x_hi, x_lo, 4 * j, 4, 512, j == 0, j == 1)
                else:
                    last = project(s, two4, x_hi, x_lo)
                last.then_inc(unit_done, 1)
                if U_VA <= unit < U_MOBA:
                    if unit == U_VA:
                        eng.wait_ge(proj_copied, COPIED[U_KI] + 1)
                    pe_dots(eng, unit - U_VA)
                if unit == U_VB + 1:
                    eng.wait_ge(v_copied, 3)
                    eng.wait_ge(dots_relu, 8)
                if apply is not None:
                    pe_apply(eng, apply)

        def pe_gates(eng):
            eng.wait_ge(conv_ready, CT)
            eng.wait_ge(wri_in, 64)
            eng.wait_ge(logits_read, A_END)
            for m in range(2):
                for c in range(CT):
                    last = mm(bank[2 * m + c // 2][:, (c % 2) * 256:(c % 2) * 256 + 256], wri[:, m, c, :],
                              conv[:, c, :], start=True, stop=True)
            last.then_inc(ri_ready, 1)
            eng.wait_ge(proj_copied, len(COPIED))
            eng.wait_ge(o_copied, A_END)
            eng.wait_ge(o_squared, A_END)
            eng.wait_ge(pt_copied2, A_END - A_MOBA)
            for c in range(6):
                for j, banks in ((0, two4), (1, two5)):
                    unit = U_GATE + 3 * c + j
                    eng.wait_ge(lo_done, unit + 1)
                    if c:
                        eng.wait_ge(gate_exp, 2 * c + j - 1)
                    project(unit % SLOTS, banks, x_hi, x_lo).then_inc(unit_done, 1)
                unit = U_GATE + 3 * c + 2
                eng.wait_ge(lo_done, unit + 1)
                if c:
                    eng.wait_ge(p_read, c)
                if c == 2:
                    eng.wait_ge(y_ready, 1)
                b = c % 3
                project(unit % SLOTS, [bank[6 + j // 2][:, (j % 2) * 256:(j % 2) * 256 + 256] for j in range(4)],
                        y_hi[:, b], y_lo[:, b], nk=4).then_inc(unit_done, 1)

        @block.tensor
        def _(eng):
            eng.wait_ge(small_in, SMALL)
            nc.tensor.transpose(bank[4][:, 0:NROWS], prow, ident[0:NROWS, 0:NROWS]).then_inc(pe_start, 1)
            mm(bank[5][0:24, 0:384], tab, onehot, start=True, stop=True).then_inc(pe_start, 1)
            eng.wait_ge(set_done, 2)
            eng.wait_ge(v_start, 1)
            mm(bank[6][:, 0:2], ones, lprod, start=True, stop=True).then_inc(pe_start, 1)
            eng.wait_ge(x_in, 16)
            eng.wait_ge(pool_in, 32)
            for k in range(KT):
                b, o, g = bank[k // 2], (k % 2) * 256, k // 2
                mm(b[:, o:o + 256], x[:, 0, k * P:(k + 1) * P], pool_m[:, g, 0:256], start=True, stop=False)
                last = mm(b[:, o + 128:o + 256], x[:, 1, k * P:(k + 1) * P], pool_m[:, g, 256:384],
                          start=False, stop=True)
            last.then_inc(pooled, 1)
            eng.wait_ge(pool_copied, 1)
            for i in range(NT):
                for g in range(NG):
                    for k in range(2):
                        last = mm(acc[i][g // 2][:, (g % 2) * 256:(g % 2) * 256 + 256],
                                  pool_d[:, 2 * g + k, i * P:(i + 1) * P], pool_w[:, g, k, :],
                                  start=(k == 0), stop=(k == 1))
            last.then_inc(mixed, 1)
            eng.wait_ge(v_start, 5)
            eng.wait_ge(s_start, 2)
            pe_norm(eng, 0, x, 1)
            pe_ffn(eng, 0)
            pe_norm(eng, 1, x, 2)
            for j in range(4):
                eng.wait_ge(lo_done, U_V + j + 1)
                rows((U_V + j) % SLOTS, acc, x_hi, x_lo, 2 * j, 2, D, j == 0, j == 3).then_inc(unit_done, 1)
            for unit, apply, score_step in HEAD_TURNS:
                if apply is not None:
                    pe_turn_probs(eng, apply)
                if score_step is not None:
                    if score_step == 0:
                        eng.wait_ge(v_copied, 1)
                    pe_score(eng, score_step, U_HEAD + score_step)
                if unit is not None:
                    eng.wait_ge(lo_done, unit + 1)
                    if COPIED[unit]:
                        eng.wait_ge(proj_copied, COPIED[unit])
                    project(unit % SLOTS, two4, x_hi, x_lo).then_inc(unit_done, 1)
                if apply is not None:
                    pe_apply(eng, apply)
            eng.wait_ge(o_copied, HEADS)
            eng.wait_ge(o_squared, HEADS)
            pe_norm(eng, 2, o1, 3)
            for j in range(4):
                eng.wait_ge(lo_done, U_WO + j + 1)
                rows((U_WO + j) % SLOTS, acc, x_hi, x_lo, 2 * j, 2, D, j == 0, j == 3).then_inc(unit_done, 1)
            pe_norm(eng, 3, x, 4)
            pe_ffn(eng, 1)
            pe_norm(eng, 4, nbuf, 5)
            pe_mixer(eng)
            pe_gates(eng)
            eng.wait_ge(x_ready, 6)
            for j in range(4):
                eng.wait_ge(lo_done, U_WO2 + j + 1)
                rows((U_WO2 + j) % SLOTS, acc, x_hi, x_lo, 2 * j, 2, D, j == 0, j == 3).then_inc(unit_done, 1)
            pe_norm(eng, 5, nbuf, 7)
            pe_mlp(eng)

        def split_views(slot, indexer):
            if indexer:
                r = raw[slot][:, 0:72 * KT].rearrange("p (k c) -> p k c", k=KT)
                return [[(o[:, :, 0:64], r[:, :, 0:64]), (o[:, :, 64:128], r[:, :, 0:64]),
                         (o[:, :, 128:136], r[:, :, 64:72])] for o in (part(w, slot, KT) for w in (w_hi, w_lo))]
            return [[(w[slot][:, :], raw[slot][:, :])] for w in (w_hi, w_lo)]

        def round_unit(eng, unit, slot, landed, fresh=False, indexer=False):
            eng.wait_ge(raw_in[slot], landed)
            if not fresh:
                eng.wait_ge(unit_done, unit - (SLOTS - 1))
            for o, i in split_views(slot, indexer)[0]:
                last = nc.scalar.activation(o, i, ACT.Copy)
            last.then_inc(hi_done, 1)

        def rest_unit(eng, unit, slot, indexer=False):
            eng.wait_ge(hi_done, unit + 1)
            his, los = split_views(slot, indexer)
            for (h, _), (o, i) in zip(his, los):
                last = nc.vector.tensor_tensor(o, i, h.bitcast(F32), ALU.subtract)
            last.then_inc(lo_done, 1)

        def s_split(eng, unit):
            if unit < U_END:
                round_unit(eng, unit, unit % SLOTS, 32 * (unit // SLOTS + 1), unit < SLOTS, unit == U_KI)

        def v_split(eng, unit):
            if unit < U_END:
                rest_unit(eng, unit, unit % SLOTS, unit == U_KI)

        def s_norm_split(eng, ev):
            for h in range(2):
                eng.wait_ge(xf_ready, 2 * ev + h + 1)
                nc.scalar.activation(x_hi[:, 4 * h:4 * h + 4, :], xf[:, 4 * h:4 * h + 4, :],
                                     ACT.Copy).then_inc(x_rounded, 1)

        hidden_rows = ffn_h.rearrange("p (a b) -> p a b", a=2)

        def s_ffn(eng, f):
            u0 = U_FFN[f]

            def exp_of(unit):
                eng.wait_ge(unit_done, unit + 1)
                nc.scalar.activation(ffn_e, bank[4][:, :], ACT.Exp, scale=-1.0).then_inc(exp_done, 1)

            def round_h(i, before):
                eng.wait_ge(up_read, i + (f * NCH + 1))
                if before is not None:
                    eng.wait_ge(unit_done, before)
                nc.scalar.activation(h_hi, hidden_rows, ACT.Copy).then_inc(h_rounded, 1)

            s_split(eng, u0 + 2)
            exp_of(u0)
            s_split(eng, u0 + 3)
            round_h(0, None)
            with eng.Fori(1, NCH) as i:
                unit = i * 3 + (u0 - 1)
                for j in range(3):
                    nxt = u0 + 4 + j
                    round_unit(eng, unit + 2 + j, nxt % SLOTS, i * 32 + (nxt // SLOTS) * 32)
                    if j == 0:
                        exp_of(unit)
                round_h(i, unit + 3)
            s_split(eng, u0 + 3 * NCH + 1)

        def s_mlp(eng):
            def relu_of(unit):
                eng.wait_ge(unit_done, unit + 1)
                nc.scalar.activation(ffn_e, bank[4][:, :], ACT.Relu).then_inc(relu_done, 1)

            def round_h(i, before):
                eng.wait_ge(sq_done, i + 1)
                if before is not None:
                    eng.wait_ge(unit_done, before)
                nc.scalar.activation(h_hi, hidden_rows, ACT.Copy).then_inc(m_rounded, 1)

            s_split(eng, U_MLP + 2)
            relu_of(U_MLP)
            round_h(0, None)
            with eng.Fori(0, (NCH2 - 1) // 3 - 1) as i:
                for j in range(3):
                    unit = i * 6 + (U_MLP + 1 + 2 * j)
                    nxt = U_MLP + 3 + 2 * j
                    round_unit(eng, unit + 2, nxt % SLOTS, i * 64 + 32 * (nxt // SLOTS + 1))
                    relu_of(unit)
                    round_unit(eng, unit + 3, (nxt + 1) % SLOTS, i * 64 + 32 * ((nxt + 1) // SLOTS + 1))
                    round_h(i * 3 + (j + 1), unit + 2)
            for c in range(NCH2 - 3, NCH2):
                unit = U_MLP + 2 * c - 1
                s_split(eng, unit + 2)
                relu_of(unit)
                s_split(eng, unit + 3)
                round_h(c, unit + 2)

        def s_softmax(eng, a):
            eng.wait_ge(logits_read, a + 1)
            if a:
                eng.wait_ge(prob_ready, a)
            for m in range(2):
                for i, c in enumerate((slice(0, P), slice(P, 384))):
                    last = nc.scalar.activation(prob_e[:, m, c], logit[:, m, c], ACT.Exp, scale=-1.0,
                                                bias=nmax[:, m, i:i + 1], accum_out=zsum[:, m, i:i + 1])
            last.then_inc(exp_ready, 1)

        def s_out_step(eng, a):
            if a < A_MOBA:
                eng.wait_ge(o_copied, a + 1)
                if a:
                    eng.wait_ge(o_squared, a)
                for i in range(NT):
                    last = nc.scalar.activation(head_scr[:, i, :], o1[:, i, a * VD:(a + 1) * VD], ACT.Square,
                                                accum_out=sumsq[:, i, a:a + 1])
            else:
                eng.wait_ge(applied, a + 1)
                b, pr = (a - A_MOBA) // 4, (a - A_MOBA) % 4
                last = nc.scalar.activation(y_hi[:, b, pr, :], bank[5][:, 0:SEQ], ACT.Copy)
            last.then_inc(o_squared, 1)

        def s_copy_unit(eng, unit):
            eng.wait_ge(unit_done, unit + 1)
            both = bank[4][:, :].rearrange("p (a b) -> p a b", a=2)
            if unit == U_KI:
                nc.scalar.activation(wi_s[:, :, :], bank[4][:, 256:272].rearrange("p (a b) -> p a b", a=2), ACT.Copy)
                nc.scalar.activation(ki, bank[4][:, 0:SEQ], ACT.Copy).then_inc(proj_copied, 1)
                return
            if step_of(unit) is not None:
                dst = qk[step_of(unit) % 2]
            elif unit < U_KI:
                dst = qi[:, 2 * (unit - U_QI):2 * (unit - U_QI) + 2, :]
            elif unit < U_DSA:
                dst = xc[:, 2 * (unit - U_XC):2 * (unit - U_XC) + 2, 3:259]
            else:
                dst = yc[:, 2 * (unit - U_YC):2 * (unit - U_YC) + 2, :]
            nc.scalar.activation(dst, both, ACT.Copy).then_inc(proj_copied, 1)

        def s_dots(eng, g):
            eng.wait_ge(dotted, g + 1)
            for m in range(2):
                if g:
                    eng.wait_ge(dots_used, 2 * g + m - 1)
                nc.scalar.activation(dots[:, m, :], bank[2 + m][:, 0:384], ACT.Relu).then_inc(dots_relu, 1)

        def s_mixer(eng):
            for unit, apply, score_step in TURNS:
                if apply is not None:
                    eng.wait_ge(turned, apply + 1)
                    if apply > A_MOBA:
                        eng.wait_ge(applied, apply)
                    for m in range(2):
                        last = nc.scalar.activation(prob_t[:, m, :], bank[6 + m][:, 0:384], ACT.Copy)
                    last.then_inc(pt_copied2, 1)
                s_split(eng, unit + 2)
                if score_step is not None:
                    s_softmax(eng, score_step)
                if unit in COPIED:
                    s_copy_unit(eng, unit)
                if unit in (U_VA + 1, U_VB + 1):
                    eng.wait_ge(unit_done, unit + 1)
                    v = v_a if unit < U_VB else v_b
                    for i in range(NT):
                        last = nc.scalar.activation(v[:, i, :], bank[i][:, :], ACT.Copy)
                    last.then_inc(v_copied, 1)
                if U_VA <= unit < U_MOBA:
                    s_dots(eng, unit - U_VA)
                if apply is not None:
                    s_out_step(eng, apply)

        def s_gates(eng):
            for c in range(6):
                for j in range(3):
                    s_split(eng, U_GATE + 3 * c + j + 2)
                    if (c, j) == (0, 0):
                        eng.wait_ge(ri_ready, 1)
                        for m, o in ((0, gr), (1, gi)):
                            for n in range(CT):
                                src = bank[2 * m + n // 2][:, (n % 2) * 256:(n % 2) * 256 + 256]
                                last = nc.scalar.activation(o[:, n, :], src, ACT.Exp, scale=-1.0,
                                                            bias=neg_b[:, 4 * m + n:4 * m + n + 1])
                            last.then_inc(ri_exp, 1)
                        eng.wait_ge(proj_copied, len(COPIED))
                        nc.scalar.activation(gl, yc, ACT.Square).then_inc(gelu_sq, 1)
                    if (c, j) == (0, 2):
                        eng.wait_ge(ri_sig, 1)
                        for n in range(CT):
                            nc.scalar.activation(rt[:, n, :], gr[:, n, :], ACT.Tanh, scale=lru_c[:, n:n + 1])
                            last = nc.scalar.activation(ra[:, n, :], gr[:, n, :], ACT.Exp, scale=lru_c[:, n:n + 1])
                        last.then_inc(lru_act, 1)
                        eng.wait_ge(gelu_z, 1)
                        nc.scalar.activation(gl, gl, ACT.Exp, scale=-GELU_B).then_inc(gelu_e, 1)
                    if (c, j) == (1, 1):
                        eng.wait_ge(lru_u2, 1)
                        nc.scalar.activation(rt, rt, ACT.Sqrt).then_inc(lru_root, 1)
                    if (c, j) == (2, 0):
                        eng.wait_ge(yc_ready, 1)
                        nc.scalar.activation(y_hi[:, 2], yc, ACT.Copy).then_inc(yc_rounded, 1)
                    if j < 2:
                        eng.wait_ge(unit_done, U_GATE + 3 * c + j + 1)
                        if c:
                            eng.wait_ge(p_read, c)
                        nc.scalar.activation(sig[:, 2 * j:2 * j + 2, :],
                                             bank[4 + j][:, :].rearrange("p (a b) -> p a b", a=2),
                                             ACT.Exp, scale=-1.0).then_inc(gate_exp, 1)

        def s_rms(eng, n):
            eng.wait_ge(z_ready, n + 1)
            for i in range(NT):
                last = nc.scalar.activation(sq_scr[:, i, :], x[:, i, :], ACT.Square, accum_out=sumsq[:, i, 0:1])
            last.then_inc(ss_ready, 1)

        @block.scalar
        def _(eng):
            for name, (row, n) in ROWS.items():
                eng.dma_start(prow[row:row + n, :], t[name]).then_inc(small_in, 16)
            for dst, src in ((onehot, t["c_onehot"]), (vecmask, t["c_vecmask"]), (ident[:, :], t["c_ident"]),
                             (causal[:, :], t["c_causal"]), (tab[:, 0:8], t["rel_table"]),
                             (tab[:, 8:24], t["rel_bias_2"])):
                eng.dma_start(dst, src).then_inc(small_in, 16)
            with nc.allow_non_contiguous_dma("256 numbers"):
                eng.dma_start(lp, t["lam_p"].rearrange("a b -> b a")).then_inc(small_in, 16)
            s_split(eng, 0)
            eng.wait_ge(v_start, 3)
            nc.scalar.activation(sp[:, 2, :], sp[:, 1, :], ACT.Exp, scale=-1.0).then_inc(s_link, 1)
            eng.wait_ge(s_link, 1)
            nc.scalar.activation(sp[:, 3, :], sp[:, 2, :], ACT.Ln, bias=1.0).then_inc(s_start, 1)
            eng.wait_ge(pe_start, 3)
            nc.scalar.activation(e_lam[:, :], bank[6][:, 0:2], ACT.Exp).then_inc(s_start, 1)
            s_split(eng, 1)
            eng.wait_ge(pooled, 1)
            for h in range(4):
                last = nc.scalar.activation(pool_d[:, 2 * h:2 * h + 2, :],
                                            bank[h][:, :].rearrange("p (a b) -> p a b", a=2), ACT.Copy)
            last.then_inc(pool_copied, 1)
            s_norm_split(eng, 0)
            s_ffn(eng, 0)
            s_norm_split(eng, 1)
            for j in range(4):
                s_split(eng, U_V + j + 2)
            eng.wait_ge(unit_done, U_V + 4)
            for i in range(NT):
                for h in range(2):
                    last = nc.scalar.activation(v1[:, i, h * 512:(h + 1) * 512], acc[i][h], ACT.Copy)
            last.then_inc(v_copied, 1)
            for unit, apply, score_step in HEAD_TURNS:
                if unit is not None:
                    s_split(eng, unit + 2)
                if score_step is not None:
                    s_softmax(eng, score_step)
                if unit is not None:
                    s_copy_unit(eng, unit)
                if apply is not None:
                    s_out_step(eng, apply)
            s_norm_split(eng, 2)
            for j in range(4):
                s_split(eng, U_WO + j + 2)
            s_norm_split(eng, 3)
            s_ffn(eng, 1)
            s_rms(eng, 0)
            s_norm_split(eng, 4)
            s_mixer(eng)
            s_gates(eng)
            eng.wait_ge(unit_done, U_WO2)
            for h in range(2):
                eng.wait_ge(merged_ready, h + 1)
                nc.scalar.activation(x_hi[:, 4 * h:4 * h + 4, :], merged[:, 4 * h:4 * h + 4, :],
                                     ACT.Copy).then_inc(x_rounded, 1)
            for j in range(4):
                s_split(eng, U_WO2 + j + 2)
            s_rms(eng, 1)
            s_norm_split(eng, 5)
            s_mlp(eng)
            s_rms(eng, 2)

        class Link:

            def __init__(self, eng, s):
                self.eng, self.s, self.n = eng, s, 0

            def __call__(self, ins):
                self.n += 1
                ins.then_inc(self.s, 1)
                self.eng.wait_ge(self.s, self.n)

        V = nc.vector
        TILE_COLS = (slice(0, P), slice(P, 384))
        TABLE_COLS = (slice(P, SEQ), slice(0, SEQ))
        var_count = [0]

        def v_var(eng, link, out_cols, src, factor, eps):
            V.tensor_scalar(vareps[:, out_cols], src, factor, eps, ALU.mult, ALU.add).then_inc(var_ready, 1)
            var_count[0] += 1
            return var_count[0]

        def v_layernorm(eng, link):
            for i in range(NT):
                for h in range(2):
                    last = V.bn_stats(stats[:, i, h, :], x[:, i, h * 512:(h + 1) * 512])
            link(last)
            for i in range(NT):
                last = V.bn_aggr(mv[:, i, :], stats[:, i, :, :])
            link(last)
            for i in range(NT):
                n = v_var(eng, link, slice(i, i + 1), mv[:, i, 1:2], 1.0, LN_EPS)
            for i in range(NT):
                eng.wait_ge(rstd_ready, n - 1 + i)
                ins = V.tensor_scalar(x[:, i, :], x[:, i, :], mv[:, i, 0:1], rstd[:, i:i + 1], ALU.subtract, ALU.mult)
                yield i, ins

        def v_transposed(eng, link, ev, gain, offset, rounds):
            eng.wait_ge(n_turned, ev + 1)
            for k in range(KT):
                src = bank[4 + k // 2][:, (k % 2) * 256:(k % 2) * 256 + 256]
                if offset:
                    last = V.tensor_scalar(xf[:, k, :], src, gain(k), offset(k), ALU.mult, ALU.add)
                else:
                    last = V.tensor_scalar(xf[:, k, :], src, gain(k), None, ALU.mult)
                if k % 4 == 3:
                    last.then_inc(xf_ready, 1)
            v_low(eng, xf, rounds)

        def v_low(eng, src, rounds):
            for h in range(2):
                eng.wait_ge(x_rounded, 2 * rounds + h + 1)
                k = slice(4 * h, 4 * h + 4)
                last = V.tensor_tensor(x_lo[:, k, :], src[:, k, :], x_hi[:, k, :].bitcast(F32), ALU.subtract)
            last.then_inc(x_ready, 1)

        def v_residual(eng, link, factor):
            for i in range(NT):
                for h in range(2):
                    c = slice(h * 512, (h + 1) * 512)
                    last = V.scalar_tensor_tensor(x[:, i, c], x[:, i, c], factor, acc[i][h], ALU.mult, ALU.add)
            return last

        def v_ln_phase(eng, link, ev, unit, nat, g, b, rounds, layer):
            eng.wait_ge(unit_done, unit + 1)
            if nat:
                eng.wait_ge(nat_ready, nat)
            link(v_residual(eng, link, ALPHA))
            for i, ins in v_layernorm(eng, link):
                ins.then_inc(n_ready, 1)
            v_transposed(eng, link, ev, lambda k: col(g, 8 * layer + k), lambda k: col(b, 8 * layer + k), rounds)

        def v_rms(eng, n_rms):
            eng.wait_ge(ss_ready, n_rms + 1)
            n = v_var(eng, None, slice(0, NT), sumsq[:, :, 0], 1.0 / D, EPS)
            eng.wait_ge(rstd_ready, n)

        def v_ffn(eng, f):
            u0 = U_FFN[f]

            def sigmoid(i):
                eng.wait_ge(exp_done, i + (f * NCH + 1))
                V.tensor_scalar(ffn_e, ffn_e, 1.0, None, ALU.add).then_inc(sig_step, 1)
                eng.wait_ge(sig_step, i * 2 + (2 * f * NCH + 1))
                V.reciprocal(ffn_e, ffn_e).then_inc(sig_step, 1)
                eng.wait_ge(sig_step, i * 2 + (2 * f * NCH + 2))
                V.tensor_tensor(ffn_t, bank[4][:, :], ffn_e, ALU.mult).then_inc(gate_read, 1)

            def hidden(i, up_unit):
                eng.wait_ge(unit_done, up_unit + 1)
                eng.wait_ge(gate_read, i + (f * NCH + 1))
                V.tensor_tensor(ffn_h, bank[5][:, :], ffn_t, ALU.mult).then_inc(up_read, 1)

            def low(i):
                eng.wait_ge(h_rounded, i + (f * NCH + 1))
                V.tensor_tensor(h_lo, ffn_h.rearrange("p (a b) -> p a b", a=2), h_hi.bitcast(F32),
                                ALU.subtract).then_inc(h_ready, 1)

            v_split(eng, u0 + 2)
            sigmoid(0)
            v_split(eng, u0 + 3)
            hidden(0, u0 + 1)
            low(0)
            with eng.Fori(1, NCH) as i:
                unit = i * 3 + (u0 - 1)
                for j in range(3):
                    rest_unit(eng, unit + 2 + j, (u0 + 4 + j) % SLOTS)
                    if j == 0:
                        sigmoid(i)
                    if j == 1:
                        hidden(i, unit + 1)
                low(i)
            v_split(eng, u0 + 3 * NCH + 1)

        def v_mlp(eng):
            def square(i, fresh=False):
                eng.wait_ge(relu_done, i + 1)
                if not fresh:
                    eng.wait_ge(m_ready, i)
                V.scalar_tensor_tensor(ffn_h, bank[4][:, :], 0.0, ffn_e, ALU.max, ALU.mult).then_inc(sq_done, 1)

            def low(i):
                eng.wait_ge(m_rounded, i + 1)
                V.tensor_tensor(h_lo, ffn_h.rearrange("p (a b) -> p a b", a=2), h_hi.bitcast(F32),
                                ALU.subtract).then_inc(m_ready, 1)

            v_split(eng, U_MLP + 2)
            square(0, True)
            low(0)
            with eng.Fori(0, (NCH2 - 1) // 3 - 1) as i:
                for j in range(3):
                    unit = i * 6 + (U_MLP + 1 + 2 * j)
                    nxt = U_MLP + 3 + 2 * j
                    rest_unit(eng, unit + 2, nxt % SLOTS)
                    square(i * 3 + (j + 1))
                    rest_unit(eng, unit + 3, (nxt + 1) % SLOTS)
                    low(i * 3 + (j + 1))
            for c in range(NCH2 - 3, NCH2):
                v_split(eng, U_MLP + 2 * c + 1)
                square(c)
                v_split(eng, U_MLP + 2 * c + 2)
                low(c)

        def v_logits(eng, link, a):
            eng.wait_ge(scored, a + 1)
            if a:
                eng.wait_ge(exp_ready, a)
            if a >= A_DSA:
                for m in range(2):
                    last = V.tensor_tensor(logit[:, m, :], bank[2 * (a % 2) + m][:, 0:384], chosen, ALU.add)
                link(last)
            for m in range(2):
                slot = a if a < A_MOBA else 8 + 2 * (a - A_MOBA) + m if a < A_DSA else 2 * (a - A_DSA) + m
                for i in range(NT):
                    c = TILE_COLS[i]
                    src = logit[:, m, c] if a >= A_DSA else bank[2 * (a % 2) + m][:, c]
                    last = V.tensor_tensor_reduce(logit[:, m, c], src, table[:, slot, TABLE_COLS[i]], -SM, 3e38,
                                                  ALU.add, ALU.min, nmax[:, m, i:i + 1])
            last.then_inc(logits_read, 1)

        def v_probs(eng, link, a):
            eng.wait_ge(exp_ready, a + 1)
            if a:
                eng.wait_ge(turned, a)
            link(V.reciprocal(rz[:, :, :], zsum[:, :, :]))
            if a < A_MOBA:
                link(V.tensor_scalar(rz[:, 1, :], rz[:, 1, :], neg_lam[:, 0:1], None, ALU.mult))
            for m in range(1 if a < A_MOBA else 2):
                for i, c in enumerate(TILE_COLS):
                    last = V.tensor_scalar(prob[:, m, c], prob_e[:, m, c], rz[:, m, i:i + 1], None, ALU.mult)
            if a < A_MOBA:
                link(last)
                for i, c in enumerate(TILE_COLS):
                    last = V.scalar_tensor_tensor(prob[:, 0, c], prob_e[:, 1, c], rz[:, 1, i:i + 1], prob[:, 0, c],
                                                  ALU.mult, ALU.add)
            last.then_inc(prob_ready, 1)

        def v_out_step(eng, a):
            if a < A_MOBA:
                eng.wait_ge(applied, a + 1)
                V.tensor_copy(o1[:, :, a * VD:(a + 1) * VD],
                              bank[5][:, 0:SEQ].rearrange("p (a b) -> p a b", a=2)).then_inc(o_copied, 1)
            else:
                b, pr = (a - A_MOBA) // 4, (a - A_MOBA) % 4
                eng.wait_ge(o_squared, a + 1)
                V.tensor_tensor(y_lo[:, b, pr, :], bank[5][:, 0:SEQ], y_hi[:, b, pr, :].bitcast(F32),
                                ALU.subtract).then_inc(o_copied, 1)

        def v_dots(eng, link, g):
            for m in range(2):
                eng.wait_ge(dots_relu, 2 * g + m + 1)
                for i, c in enumerate(TILE_COLS):
                    w = wi_s[:, i, 2 * g + m:2 * g + m + 1]
                    if g == 0 and m == 0:
                        last = V.tensor_scalar(score[:, c], dots[:, m, c], w, None, ALU.mult)
                    else:
                        last = V.scalar_tensor_tensor(score[:, c], dots[:, m, c], w, score[:, c], ALU.mult, ALU.add)
                last.then_inc(dots_used, 1)
                eng.wait_ge(dots_used, 2 * g + m + 1)
            if g == 3:
                for i, c in enumerate(TILE_COLS):
                    last = V.scalar_tensor_tensor(work[:, c], score[:, c], IDX_SCALE, causal[:, TABLE_COLS[i]],
                                                  ALU.mult, ALU.add)
                link(last)

        def v_topk_round(eng, link):
            for i, c in enumerate(TILE_COLS):
                last = V.max(top8[:, i, :], work[:, c])
            link(last)
            for i, c in enumerate(TILE_COLS):
                last = V.match_replace(work[:, c], top8[:, i, :], work[:, c], TAKEN)
            link(last)

        def v_conv(eng, link, n):
            eng.wait_ge(proj_copied, COPIED[U_XC + 1] + 1)
            eng.wait_ge(set_done, 3)
            o = conv[:, n, :]
            link(V.tensor_scalar(o, xc[:, n, 3:259], col("conv_w_2", 12 + n), col("conv_b_2", n), ALU.mult, ALU.add))
            for tap in (2, 1, 0):
                ins = V.scalar_tensor_tensor(o, xc[:, n, tap:tap + 256], col("conv_w_2", 4 * tap + n), o,
                                             ALU.mult, ALU.add)
                if tap:
                    link(ins)
            ins.then_inc(conv_ready, 1)

        def v_mixer(eng, link):
            for unit, apply, score_step in TURNS:
                if score_step is not None:
                    if score_step == A_DSA:
                        eng.wait_ge(table2_in, 16)
                    v_logits(eng, link, score_step)
                v_split(eng, unit + 2)
                if score_step is not None:
                    v_probs(eng, link, score_step)
                if U_VA <= unit < U_MOBA:
                    v_dots(eng, link, unit - U_VA)
                if U_MOBA - 1 <= unit < U_MOBA - 1 + TOPK // 8:
                    v_topk_round(eng, link)
                if unit == U_MOBA - 2 + TOPK // 8:
                    link(V.tensor_scalar(chosen, work, -2e38, NEG, ALU.is_gt, ALU.mult))
                if U_DSA <= unit < U_DSA + CT:
                    v_conv(eng, link, unit - U_DSA)
                if apply is not None:
                    v_out_step(eng, apply)

        def v_gates(eng, link):
            for c in range(6):
                half, b = c // 3, c % 3
                for j in range(3):
                    v_split(eng, U_GATE + 3 * c + j + 2)
                    if (c, j) == (0, 1):
                        for m, o in ((0, gr), (1, gi)):
                            eng.wait_ge(ri_exp, m + 1)
                            link(V.tensor_scalar(o, o, 1.0, None, ALU.add))
                            ins = V.reciprocal(o, o)
                            if m == 0:
                                ins.then_inc(ri_sig, 1)
                            else:
                                link(ins)
                        eng.wait_ge(gelu_sq, 1)
                        link(V.tensor_scalar(gl, gl, GELU_A, 1.0, ALU.mult, ALU.add))
                        V.tensor_tensor(gl, gl, yc, ALU.mult).then_inc(gelu_z, 1)
                    if (c, j) == (1, 0):
                        eng.wait_ge(lru_act, 1)
                        link(V.tensor_scalar(rq, rt, -1.0, 1.0, ALU.mult, ALU.add))
                        link(V.reciprocal(rq, rq))
                        link(V.scalar_tensor_tensor(rt, rt, -2.0, rq, ALU.mult, ALU.mult))
                        V.tensor_scalar(rt, rt, ROOT_MIN, None, ALU.max).then_inc(lru_u2, 1)
                        link(V.tensor_tensor(gi, gi, conv, ALU.mult))
                    if (c, j) == (1, 1):
                        eng.wait_ge(gelu_e, 1)
                        link(V.tensor_scalar(gl, gl, 1.0, None, ALU.add))
                        link(V.reciprocal(gl, gl))
                        link(V.tensor_tensor(yc, yc, gl, ALU.mult))
                    if (c, j) == (1, 2):
                        eng.wait_ge(lru_root, 1)
                        link(V.tensor_tensor(rt, rt, gi, ALU.mult))
                        for n in range(CT):
                            last = V.tensor_tensor_scan(gr[:, n, :], ra[:, n, :], rt[:, n, :], 0.0, ALU.mult, ALU.add)
                        link(last)
                        V.tensor_tensor(yc, yc, gr, ALU.mult).then_inc(yc_ready, 1)
                    if (c, j) == (2, 0):
                        eng.wait_ge(yc_rounded, 1)
                        V.tensor_tensor(y_lo[:, 2], yc, y_hi[:, 2].bitcast(F32), ALU.subtract).then_inc(y_ready, 1)
                    if j < 2:
                        s = sig[:, 2 * j:2 * j + 2, :]
                        eng.wait_ge(gate_exp, 2 * c + j + 1)
                        link(V.tensor_scalar(s, s, 1.0, None, ALU.add))
                        link(V.reciprocal(s, s))
                    else:
                        eng.wait_ge(unit_done, U_GATE + 3 * c + 3)
                        m = merged[:, 4 * half:4 * half + 4, :]
                        o = m if b == 0 else prod
                        for n in range(2):
                            last = V.tensor_tensor(o[:, 2 * n:2 * n + 2, :],
                                                   bank[6 + n][:, :].rearrange("p (a b) -> p a b", a=2),
                                                   sig[:, 2 * n:2 * n + 2, :], ALU.mult)
                        last.then_inc(p_read, 1)
                        eng.wait_ge(p_read, c + 1)
                        if b:
                            ins = V.tensor_tensor(m, m, prod, ALU.add)
                            if b == 1:
                                link(ins)
                            else:
                                ins.then_inc(merged_ready, 1)

        @block.vector
        def _(eng):
            link = Link(eng, v_link)
            eng.wait_ge(small_in, SMALL)
            V.tensor_tensor(lprod, lp[:, 0:4:2], lp[:, 1:4:2], ALU.mult).then_inc(v_start, 1)
            eng.wait_ge(pe_start, 1)
            V.tensor_copy(par[:, :], bank[4][:, 0:NROWS]).then_inc(v_start, 1)
            eng.wait_ge(v_start, 2)
            lam = par[:, ROWS["lru_lambda_2"][0]:ROWS["lru_lambda_2"][0] + CT]
            link(V.tensor_scalar(sp[:, 0, :], lam, -1.0, None, ALU.mult))
            V.tensor_tensor(sp[:, 1, :], sp[:, 0, :], lam, ALU.max).then_inc(v_start, 1)
            eng.wait_ge(pe_start, 2)
            V.scalar_tensor_tensor(vec, bank[5][0:24, 0:384], 1.0 / SM, vecmask, ALU.mult, ALU.add).then_inc(v_start, 1)
            b0 = ROWS["b_r_2"][0]
            V.tensor_scalar(neg_b[:, :], par[:, b0:b0 + 8], -1.0, None, ALU.mult)
            V.tensor_scalar(sub_gain[:, :], col("subln_g"), 1.0 - LAMBDA_INIT, None, ALU.mult)
            eng.wait_ge(s_start, 1)
            link(V.scalar_tensor_tensor(sp[:, 0, :], sp[:, 0, :], 0.0, sp[:, 3, :], ALU.max, ALU.add))
            V.tensor_scalar(lru_c[:, :], sp[:, 0, :], -LRU_C, None, ALU.mult)
            eng.wait_ge(s_start, 2)
            link(V.tensor_tensor(neg_lam[:, :], e_lam[:, 1:2], e_lam[:, 0:1], ALU.subtract))
            link(V.tensor_scalar(neg_lam[:, :], neg_lam[:, :], LAMBDA_INIT, None, ALU.subtract))
            v_split(eng, 0)
            v_split(eng, 1)
            eng.wait_ge(mixed, 1)
            eng.wait_ge(gb_in, 16)
            tmp = view(4096, NT, D)
            for i in range(NT):
                for h in range(2):
                    c = slice(h * 512, (h + 1) * 512)
                    last = V.tensor_tensor(tmp[:, i, c], acc[i][h], gb[:, 0, c], ALU.mult)
            last.then_inc(gb_used, 1)
            eng.wait_ge(gb_used, 1)
            link(V.scalar_tensor_tensor(x[:, :, :], x[:, :, :], ALPHA, tmp, ALU.mult, ALU.add))
            V.tensor_copy(neg_lam[:, :], neg_lam[:, :]).then_inc(v_start, 1)
            for i, ins in v_layernorm(eng, link):
                ins.then_inc(n_ready, 1)
            v_transposed(eng, link, 0, lambda k: col("ln_mix_g", k), lambda k: col("ln_mix_b", k), 0)
            v_ffn(eng, 0)
            v_ln_phase(eng, link, 1, U_V - 1, 1, "ln_ffn_g", "ln_ffn_b", 1, 0)
            for j in range(4):
                v_split(eng, U_V + j + 2)
            eng.wait_ge(table_in, 32)
            for unit, apply, score_step in HEAD_TURNS:
                if apply is not None:
                    eng.wait_ge(turned, apply + 1)
                    if apply:
                        eng.wait_ge(applied, apply)
                    V.tensor_copy(prob_t[:, 0, :], bank[6][:, 0:384]).then_inc(pt_copied, 1)
                if score_step is not None:
                    v_logits(eng, link, score_step)
                if unit is not None:
                    v_split(eng, unit + 2)
                if score_step is not None:
                    v_probs(eng, link, score_step)
                if apply is not None:
                    v_out_step(eng, apply)
            eng.wait_ge(o_squared, HEADS)
            n = v_var(eng, link, slice(0, 16), sumsq[:, :, :].rearrange("p a b -> p (a b)"), 1.0 / VD, LN_EPS)
            eng.wait_ge(rstd_ready, n)
            eng.wait_ge(o_copied, HEADS)
            for i in range(NT):
                o = o1[:, i, :].rearrange("p (h v) -> p h v", h=HEADS)
                r = rstd[:, i * HEADS:(i + 1) * HEADS].unsqueeze(2).broadcast_to([P, HEADS, VD])
                V.tensor_tensor(o, o, r, ALU.mult).then_inc(n_ready, 1)
            v_transposed(eng, link, 2, lambda k: sub_gain[:, 0:1], None, 2)
            for j in range(4):
                v_split(eng, U_WO + j + 2)
            v_ln_phase(eng, link, 3, U_FFN[1] - 1, 2, "ln_mix_g", "ln_mix_b", 3, 1)
            v_ffn(eng, 1)
            eng.wait_ge(unit_done, U_QI)
            eng.wait_ge(nat_ready, 3)
            link(v_residual(eng, link, ALPHA))
            for i, ins in v_layernorm(eng, link):
                link(ins)
            eng.wait_ge(gb_in, 16 * 9)
            for i in range(NT):
                last = V.tensor_tensor(x[:, i, :], x[:, i, :], gb[:, 0, :], ALU.mult)
            link(last)
            for i in range(NT):
                last = V.tensor_tensor(x[:, i, :], x[:, i, :], gb[:, 1, :], ALU.add)
            last.then_inc(z_ready, 1)
            v_rms(eng, 0)
            for i in range(NT):
                V.tensor_scalar(nbuf[:, i, :], x[:, i, :], rstd[:, i:i + 1], None, ALU.mult).then_inc(n_ready, 1)
            v_transposed(eng, link, 4, lambda k: col("norm_mix_g_2", k), None, 4)
            v_mixer(eng, link)
            v_gates(eng, link)
            v_low(eng, merged, 5)
            for j in range(4):
                v_split(eng, U_WO2 + j + 2)
            eng.wait_ge(unit_done, U_MLP)
            v_residual(eng, link, 1.0).then_inc(z_ready, 1)
            v_rms(eng, 1)
            for i in range(NT):
                V.tensor_scalar(nbuf[:, i, :], x[:, i, :], rstd[:, i:i + 1], None, ALU.mult).then_inc(n_ready, 1)
            v_transposed(eng, link, 5, lambda k: col("norm_mlp_g_2", k), None, 6)
            v_mlp(eng)
            eng.wait_ge(unit_done, U_END)
            v_residual(eng, link, 1.0).then_inc(z_ready, 1)
            v_rms(eng, 2)
            eng.wait_ge(gb_in, 16 * 10)
            for i in range(NT):
                V.scalar_tensor_tensor(x[:, i, :], x[:, i, :], rstd[:, i:i + 1], gb[:, 0, :], ALU.mult,
                                       ALU.mult).then_inc(out_ready, 1)

        @block.gpsimd
        def _(eng):
            G = nc.gpsimd

            def load_gb(*names_layers):
                for r, (name, k) in enumerate(names_layers):
                    src = t[name].rearrange("a b -> (a b)")[k * D:(k + 1) * D]
                    eng.dma_start(gb[:, r, :], src.partition_broadcast(P)).then_inc(gb_in, 16)

            def roots(n, cols, done=[0]):
                for _ in range(n):
                    at = slice(done[1], done[1] + cols) if n > 1 else slice(0, cols)
                    eng.wait_ge(var_ready, done[0] + 1)
                    G.tensor_tensor(rstd[:, at], vareps[:, at], minus_half[:, 0:1].broadcast_to([P, cols]), ALU.pow)\
                        .then_inc(rstd_ready, 1)
                    done[0] += 1
                    done[1] += cols

            done = [0, 0]

            def ln_roots():
                done[1] = 0
                roots(NT, 1, done)

            def natural(ev, loaded):
                eng.wait_ge(n_turned, ev + 1)
                eng.wait_ge(gb_in, loaded)
                for i in range(NT):
                    last = G.tensor_tensor(x[:, i, :], x[:, i, :], gb[:, 0, :], ALU.mult)
                last.then_inc(nat_link, 1)
                nat[0] += 1
                eng.wait_ge(nat_link, 2 * nat[0] - 1)
                for i in range(NT):
                    last = G.tensor_tensor(x[:, i, :], x[:, i, :], gb[:, 1, :], ALU.add)
                last.then_inc(nat_link, 1)
                eng.wait_ge(nat_link, 2 * nat[0])
                eng.sem_inc(nat_ready, 1)

            nat = [0]
            G.memset(ones, 1.0).then_inc(set_done, 1)
            G.memset(minus_half[:, :], -0.5).then_inc(set_done, 1)
            load_gb(("pool_scale", 0))
            eng.wait_ge(v_start, 4)
            eng.dma_start(vec_dram, vec.unsqueeze(1).broadcast_to([24, P, 384])).then_inc(vec_out, 16)
            eng.wait_ge(vec_out, 16)

            def toeplitz(slot, head, n=8):
                src = bass.AP(vec_dram.tensor, vec_dram.offset + head * P * 384 + 127,
                              [[383, P], [P * 384, n], [1, SEQ]])
                return eng.dma_start(table[:, slot:slot + n, :], src)

            toeplitz(0, 0).then_inc(table_in, 16)
            toeplitz(8, 8).then_inc(table_in, 16)
            eng.wait_ge(gb_used, 1)
            load_gb(("ln_mix_g", 0), ("ln_mix_b", 0))
            eng.wait_ge(pe_start, 3)
            eng.wait_ge(v_start, 5)
            G.memset(wri, 0.0).then_inc(wri_zero, 1)
            eng.wait_ge(wri_zero, 1)
            for m, name in enumerate(("w_r_2", "w_i_2")):
                for e in range(2):
                    r = slice(e * DH, (e + 1) * DH)
                    eng.dma_start(wri[r, m, :, r], t[name][e:8:2].rearrange("n c d -> c n d")).then_inc(wri_in, 16)
            ln_roots()
            natural(0, 48)
            load_gb(("ln_ffn_g", 0), ("ln_ffn_b", 0))
            ln_roots()
            natural(1, 80)
            load_gb(("ln_mix_g", 1), ("ln_mix_b", 1))
            eng.wait_ge(logits_read, HEADS)
            toeplitz(0, 16).then_inc(table2_in, 16)
            roots(1, 16, done)
            ln_roots()
            natural(3, 112)
            load_gb(("ln_ffn_g", 1), ("ln_ffn_b", 1))
            ln_roots()
            roots(1, NT, done)
            load_gb(("final_norm_g_2", 0))
            eng.wait_ge(x_ready, 5)
            G.memset(xc[:, :, 0:3], 0.0).then_inc(set_done, 1)
            roots(1, NT, done)
            roots(1, NT, done)


def kernel(**inputs):
    import concourse.bacc as bacc
    from concourse.bass_utils import run_bass_kernel_spmd

    nc = bacc.Bacc("TRN2", target_bir_lowering=False, num_devices=1)
    arrays = {k: np.ascontiguousarray(v) for k, v in inputs.items()}
    arrays.update(constants())
    t = {k: nc.dram_tensor(k, v.shape, mybir.dt.from_np(v.dtype), kind="ExternalInput").ap()
         for k, v in arrays.items()}
    for k in ("x", "pool_w", "w_qkv", "w_o", "lam_p", "w_in_2", "w_r_2", "w_i_2", "w_pa_2", "w_pb_2", "w_pc_2",
              "w_o_2", "w_up_2", "w_down_2", "conv_w_2"):
        t[k] = t[k][0]
    rows_of = dict(t)
    for k in ROWS:
        v = t[k]
        if len(v.shape) == 1:
            v = v.rearrange("(a b) -> a b", b=P)
        else:
            v = v.rearrange("a (c b) -> (a c) b", b=P)
        rows_of[k] = v
    rows_of["pool_scale"] = t["pool_scale"]
    rows_of["final_norm_g_2"] = t["final_norm_g_2"].rearrange("(a b) -> a b", a=1)
    out = nc.dram_tensor("out", (SEQ, D), F32, kind="ExternalOutput").ap()
    build(nc, rows_of, out)
    r = run_bass_kernel_spmd(nc, [arrays], core_ids=[0])
    return r.results[0]["out"].reshape(1, SEQ, D)
```

```python
import math
from contextlib import ExitStack

import numpy as np

import concourse.bass as bass
from concourse import mybir

F32 = mybir.dt.float32
F32R = mybir.dt.float32r
ALU = mybir.AluOpType
ACT = mybir.ActivationFunctionType

P = 128
SEQ = 256
NT = SEQ // P
D = 1024
KT = D // P
DFF = 2816
DFF2 = 4096
DEPTH = 2
ALPHA = (2.0 * DEPTH) ** 0.25
LN_EPS = 1e-5
EPS = 1e-6
WINDOWS = (2, 4, 8, 16)
NG = len(WINDOWS)
REACH = max(WINDOWS)
HEADS = 8
DH = 64
VD = 128
LAMBDA_INIT = 0.8 - 0.6 * math.exp(-0.3)
NBUCK = 32
MAXD = 128
D_RNN = 512
CT = D_RNN // P
LRU_C = 8.0
TOPK = SEQ // 4
IDX_HEADS = 8
IDX_SCALE = IDX_HEADS ** -0.5 * DH ** -0.5
SM = DH ** -0.5
NEG = -1e30
TAKEN = -3e38
ROOT_MIN = 2.0 ** -116
GELU_A = 0.044715
GELU_B = math.sqrt(2.0 / math.pi)

(O_QA, O_KA, O_VA, O_QB, O_KB, O_VB, O_QI, O_KI, O_WI, O_XC, O_YC, O_GT) = (
    0, 512, 1024, 1536, 2048, 2560, 3072, 3584, 3648, 3656, 4168, 4680)
D_IN = 7752

UW = 2048
SLOTS = 3
CH = 256
NCH = DFF // CH
NCH2 = DFF2 // CH
U_FFN = [0, 0]
U_FFN[0] = 0
U_V = U_FFN[0] + 3 * NCH
U_HEAD = U_V + 4
U_WO = U_HEAD + HEADS
U_FFN[1] = U_WO + 4
U_QI = U_FFN[1] + 3 * NCH
U_KI = U_QI + 2
U_VA = U_KI + 1
U_VB = U_VA + 2
U_MOBA = U_VB + 2
U_XC = U_MOBA + 4
U_DSA = U_XC + 2
U_YC = U_DSA + 4
U_GATE = U_YC + 2
U_WO2 = U_GATE + 18
U_MLP = U_WO2 + 4
U_END = U_MLP + 2 * NCH2

A_MOBA, A_DSA, A_END = 8, 12, 16


BANK5 = (U_HEAD + 1, U_QI + 1, U_MOBA + 1)


def step_of(unit):
    if U_HEAD <= unit < U_HEAD + 8:
        return unit - U_HEAD
    if U_MOBA <= unit < U_MOBA + 4:
        return A_MOBA + unit - U_MOBA
    if U_DSA <= unit < U_DSA + 4:
        return A_DSA + unit - U_DSA
    return None


def mixer_turns():
    turns = []
    started, scored, applied = A_MOBA, A_MOBA, A_MOBA
    for unit in range(U_QI, U_GATE):
        apply = applied if applied < scored else None
        score = scored if scored < started else None
        applied += apply is not None
        scored += score is not None
        started += step_of(unit) is not None
        turns.append((unit, apply, score))
    assert applied == scored == started == A_END
    return turns


TURNS = mixer_turns()
HEAD_TURNS = [(U_HEAD + i if i < 8 else None, i - 2 if i >= 2 else None, i - 1 if 1 <= i <= 8 else None)
              for i in range(10)]

V_NORM, O_NORM = 1, 2

COPIED = {}
for _u in (*range(U_HEAD, U_HEAD + 8), *range(U_QI, U_KI + 1), *range(U_MOBA, U_GATE)):
    COPIED[_u] = len(COPIED)

CHUNKS = [(0, 0), (0, 1), (1, 0), (1, 1), (0, 2), (1, 2)]

ROWS = {}
_row = 0
for _name, _n in (("ln_mix_g", 16), ("ln_mix_b", 16), ("ln_ffn_g", 16), ("ln_ffn_b", 16), ("norm_mix_g_2", 8),
                  ("norm_mlp_g_2", 8), ("conv_b_2", 4), ("b_r_2", 4), ("b_i_2", 4), ("lru_lambda_2", 4),
                  ("conv_w_2", 16), ("subln_g", 1)):
    ROWS[_name] = (_row, _n)
    _row += _n
NROWS = _row


def buckets():
    rel = 255 - np.arange(384)
    n = np.maximum(rel, 0)
    nf = np.maximum(n, 1).astype(np.float32)
    large = 16 + (np.log(nf / np.float32(16)) / np.float32(math.log(MAXD / 16)) * np.float32(16)).astype(np.int32)
    b = np.where(n < 16, n, np.minimum(large, NBUCK - 1))
    one = ((b[None] == np.arange(NBUCK)[:, None]) & (rel >= 0)[None]).astype(np.float32)
    mask = np.broadcast_to(np.where(rel >= 0, 0.0, NEG / SM).astype(np.float32), (24, 384))
    return one, np.ascontiguousarray(mask)


def pool_matrices():
    m = np.zeros((P, NG, P + REACH + P), np.float32)
    for g, w in enumerate(WINDOWS):
        full = np.zeros((SEQ, SEQ), np.float32)
        for t in range(SEQ):
            full[max(0, t + 1 - w):t + 1, t] = np.float32(1.0) / np.float32(min(t + 1, w))
        full -= np.eye(SEQ, dtype=np.float32)
        m[:, g, 0:P + REACH] = full[0:P, 0:P + REACH]
        m[:, g, P + REACH:] = full[P:, P:]
    return m


def constants():
    one, mask = buckets()
    causal = np.zeros((P, 256), np.float32)
    causal[:, 128:] = np.triu(np.full((P, P), NEG, np.float32), 1)
    return {"c_onehot": one, "c_vecmask": mask, "c_pool": pool_matrices(), "c_causal": causal,
            "c_ident": np.eye(P, dtype=np.float32)}


def build(nc, t, out):
    with ExitStack() as ctx:
        def sb(name, shape, dt=F32):
            return ctx.enter_context(nc.sbuf_tensor(name, shape, dt))

        def sem(name):
            return ctx.enter_context(nc.semaphore(name))

        raw = [sb(f"raw{s}", [P, UW]) for s in range(SLOTS)]
        w_hi = [sb(f"w_hi{s}", [P, UW], F32R) for s in range(SLOTS)]
        w_lo = [sb(f"w_lo{s}", [P, UW], F32R) for s in range(SLOTS)]
        x = sb("x_rows", [P, NT, D])
        x_hi = sb("x_hi", [P, KT, SEQ], F32R)
        x_lo = sb("x_lo", [P, KT, SEQ], F32R)
        table = sb("table", [P, 16, SEQ])
        gb = sb("gb", [P, 2, D])
        ident = sb("ident", [P, P])
        causal = sb("causal", [P, SEQ])
        par = sb("par", [P, NROWS])
        gate_b = sb("gate_b", [P, 8])
        lru_c = sb("lru_c", [P, 2 * CT])
        sp = sb("sp", [P, 4, CT])
        neg_lam = sb("neg_lam", [P, 1])
        e_lam = sb("e_lam", [P, 2])
        sub_gain = sb("sub_gain", [P, 1])
        wi_t = sb("wi_t", [IDX_HEADS, SEQ])
        wi_s = sb("wi_s", [P, NT, IDX_HEADS])
        stats = sb("stats", [P, NT, 2, 6])
        mv = sb("mv", [P, NT, 2])
        vareps = sb("vareps", [P, 16])
        rstd = sb("rstd", [P, 16])
        minus_half = sb("minus_half", [P, 1])
        nmax = sb("nmax", [P, 2, 2])
        zsum = sb("zsum", [P, 2, 2])
        rz = sb("rz", [P, 2, 2])
        sumsq = sb("sumsq", [P, 2, HEADS])
        top8 = sb("top8", [P, 2, 8])
        arena = sb("arena", [P, 13728])
        arena_r = sb("arena_r", [P, 6144], F32R)

        def view(at, *dims):
            n = int(np.prod(dims))
            v = arena[:, at:at + n]
            if len(dims) == 2:
                v = v.rearrange("p (a b) -> p a b", a=dims[0])
            if len(dims) == 3:
                v = v.rearrange("p (a b c) -> p a b c", a=dims[0], b=dims[1])
            return v

        ffn_e, ffn_t, ffn_h = view(0, 512), view(512, 512), view(1024, 512)
        h_hi, h_lo = ([arena_r[:, at + 1024 * j:at + 1024 * j + 512].rearrange("p (a b) -> p a b", a=2)
                       for j in range(2)] for at in (0, 512))
        pool_m, pool_w, pool_d = view(0, NG, 2 * P + REACH), view(2048, NG, 2, 256), view(4096, KT, SEQ)
        onehot, vecmask, vec, tab = (arena[0:32, 12288:12672], arena[0:24, 12672:13056], arena[0:24, 13056:13440],
                                     arena[0:32, 13440:13464])
        lp, lprod, ones = arena[0:64, 13464:13468], arena[0:64, 13468:13470], arena[0:64, 13472:13600]
        prow = arena[0:NROWS, 13600:13728]
        xf, nbuf = view(8192, KT, SEQ), view(10240, NT, D)
        v1, o1 = view(0, NT, D), view(2048, NT, D)
        qk = [view(4096 + 512 * i, 2, SEQ) for i in range(2)]
        logit, prob_e, prob, prob_t = view(5120, 2, 384), view(5888, 2, 384), view(6656, 2, 384), view(7424, 2, 384)
        v_a, v_b = view(0, NT, 512), view(1024, NT, 512)
        qi, ki, dots = view(2048, 4, SEQ), view(3072, SEQ), view(3328, 2, 384)
        score, work, chosen = view(8192, 384), view(8576, 384), view(8960, 384)
        y_hi = arena_r[:, 0:3072].rearrange("p (b k n) -> p b k n", b=3, k=4)
        y_lo = arena_r[:, 3072:6144].rearrange("p (b k n) -> p b k n", b=3, k=4)
        xc, conv, yc, wri = view(9344, CT, 260), view(10384, CT, SEQ), view(11408, CT, SEQ), view(12432, 2, CT, P)
        gr, gi, ra, rt = (view(4096 + 1024 * i, CT, SEQ) for i in range(4))
        rq, gl = view(12432, CT, SEQ), view(8192, CT, SEQ)
        head_scr, sq_scr = view(10240, NT, P), nbuf
        merged, sig, prod = view(0, KT, SEQ), view(2048, 4, SEQ), view(3072, 4, SEQ)

        bank = [ctx.enter_context(nc.psum_tensor(f"bank{i}", [P, 512], F32)) for i in range(8)]
        vec_dram = nc.dram_tensor("bias_vectors", (24, P, 384), F32, kind="Internal").ap()

        raw_in = [sem(f"raw_in{s}") for s in range(SLOTS)]
        hi_done = sem("hi_done")
        lo_done = sem("lo_done")
        unit_done = sem("unit_done")
        gate_read = sem("gate_read")
        up_read = sem("up_read")
        tanh_done = sem("tanh_done")
        h_rounded = sem("h_rounded")
        h_ready = sem("h_ready")
        relu_done = sem("relu_done")
        sq_done = sem("sq_done")
        m_rounded = sem("m_rounded")
        m_ready = sem("m_ready")
        x_in = [sem(f"x_in{i}") for i in range(NT)]
        small_in = sem("small_in")
        pool_m_in = sem("pool_m_in")
        pool_w_in = sem("pool_w_in")
        vec_out = sem("vec_out")
        table_in = sem("table_in")
        table2_in = sem("table2_in")
        gb_in = sem("gb_in")
        wri_in = sem("wri_in")
        set_done = sem("set_done")
        wri_zero = sem("wri_zero")
        pe_start = sem("pe_start")
        v_start = sem("v_start")
        s_start = sem("s_start")
        pooled = sem("pooled")
        pool_copied = sem("pool_copied")
        pool_scaled = sem("pool_scaled")
        mixed = sem("mixed")
        rows_done = sem("rows_done")
        v_link = sem("v_link")
        s_link = sem("s_link")
        var_ready = sem("var_ready")
        rstd_ready = sem("rstd_ready")
        ss_ready = sem("ss_ready")
        z_ready = sem("z_ready")
        n_ready = sem("n_ready")
        n_turned = sem("n_turned")
        xf0_ready = sem("xf0_ready")
        xf1_ready = sem("xf1_ready")
        x_rounded = sem("x_rounded")
        x_ready = sem("x_ready")
        x0_ready = sem("x0_ready")
        nat_ready = sem("nat_ready")
        nat_link = sem("nat_link")
        v_copied = sem("v_copied")
        proj_copied = sem("proj_copied")
        scored = sem("scored")
        logits_read = sem("logits_read")
        exp_ready = sem("exp_ready")
        prob_ready = sem("prob_ready")
        turned = sem("turned")
        pt_copied = sem("pt_copied")
        pt_copied2 = sem("pt_copied2")
        applied = sem("applied")
        o_copied = sem("o_copied")
        o_squared = sem("o_squared")
        wi_turned = sem("wi_turned")
        dotted = sem("dotted")
        dots_relu = sem("dots_relu")
        dots_used = sem("dots_used")
        conv_ready = sem("conv_ready")
        ri_ready = sem("ri_ready")
        ri_act = sem("ri_act")
        ri_sig = sem("ri_sig")
        lru_act = sem("lru_act")
        lru_u2 = sem("lru_u2")
        lru_root = sem("lru_root")
        gelu_sq = sem("gelu_sq")
        gelu_z = sem("gelu_z")
        gelu_t = sem("gelu_t")
        yc_ready = sem("yc_ready")
        yc_rounded = sem("yc_rounded")
        y_ready = sem("y_ready")
        gate_act = sem("gate_act")
        p_read = sem("p_read")
        merged_ready = sem("merged_ready")
        merged_rounded = sem("merged_rounded")
        out_ready = sem("out_ready")
        stored = sem("stored")

        block = ctx.enter_context(nc.Block())

        def half(h):
            return slice(h * 512, (h + 1) * 512)

        def col(name, k=0):
            at = ROWS[name][0] + k
            return par[:, at:at + 1]

        SMALL = 16 * (len(ROWS) + 7)

        def cols(name, k):
            at = ROWS[name][0] + k
            return par[:, at:at + 4]

        def part(tile, slot, a):
            return tile[slot][:, :].rearrange("p (a b) -> p a b", a=a)

        def by_rows(w, k0, nk, c0, nc_):
            return w[k0 * P:(k0 + nk) * P, c0:c0 + nc_].rearrange("(k p) c -> p k c", p=P)

        def load(eng, unit, slot, parts, waits=True):
            if waits:
                eng.wait_ge(lo_done, unit - (SLOTS - 1))
            for dst, src in parts:
                eng.dma_start(dst, src).then_inc(raw_in[slot], 16)

        def halved(slot, src):
            a, b = src.shape[1:]
            dst = raw[slot][:, 0:a * b].rearrange("p (a b) -> p a b", a=a)
            return [(dst[:, h * a // 2:(h + 1) * a // 2, :], src[:, h * a // 2:(h + 1) * a // 2, :]) for h in (0, 1)]

        def load_unit(eng, unit, src):
            load(eng, unit, unit % SLOTS, halved(unit % SLOTS, src), unit >= SLOTS)

        def load_heads(eng, unit, w, q0, k0):
            dst = part(raw, unit % SLOTS, KT)
            load(eng, unit, unit % SLOTS, [(dst[:, :, h * P:(h + 1) * P], by_rows(w, 0, KT, c, P))
                                           for h, c in enumerate((q0, k0))])

        def load_ffn(eng, f):
            u0 = U_FFN[f]
            gate, up, down = t["w_gate"][f], t["w_up"][f], t["w_down"][f]
            load_unit(eng, u0, by_rows(gate, 0, KT, 0, CH))
            load_unit(eng, u0 + 1, by_rows(up, 0, KT, 0, CH))
            first = 1
            if u0 == 0:
                load_unit(eng, 2, by_rows(gate, 0, KT, CH, CH))
                load_unit(eng, 3, by_rows(up, 0, KT, CH, CH))
                load_unit(eng, 4, by_rows(down, 0, 2, 0, D))
                first = 2
            slots = [(u0 + 2 + j) % SLOTS for j in range(3)]
            with eng.Fori(first, NCH) as i:
                unit = i * 3 + (u0 - 1)
                for j, w in ((0, gate), (1, up)):
                    load(eng, unit + j, slots[j],
                         halved(slots[j], w[:, bass.ds(i * CH, CH)].rearrange("(k p) c -> p k c", p=P)))
                load(eng, unit + 2, slots[2],
                     halved(slots[2], down[bass.ds(i * CH - CH, CH), :].rearrange("(k p) c -> p k c", p=P)))
            load_unit(eng, u0 + 3 * NCH - 1, by_rows(down, DFF // P - 2, 2, 0, D))

        def load_mlp(eng):
            up, down = t["w_up_2"], t["w_down_2"]
            load_unit(eng, U_MLP, by_rows(up, 0, KT, 0, CH))
            slots = [(U_MLP + 1 + j) % SLOTS for j in range(6)]
            with eng.Fori(0, (NCH2 - 1) // 3) as i:
                for j in range(3):
                    unit = i * 6 + (U_MLP + 1 + 2 * j)
                    load(eng, unit, slots[2 * j], halved(
                        slots[2 * j], up[:, bass.ds(i * (3 * CH) + (j + 1) * CH, CH)].rearrange(
                            "(k p) c -> p k c", p=P)))
                    load(eng, unit + 1, slots[2 * j + 1], halved(
                        slots[2 * j + 1], down[bass.ds(i * (3 * CH) + j * CH, CH), :].rearrange(
                            "(k p) c -> p k c", p=P)))
            load_unit(eng, U_END - 1, by_rows(down, DFF2 // P - 2, 2, 0, D))

        @block.sync
        def _(eng):
            eng.dma_start(pool_m, t["c_pool"]).then_inc(pool_m_in, 16)
            for i in range(NT):
                eng.dma_start(x[:, i, :], t["x"][i * P:(i + 1) * P, :]).then_inc(x_in[i], 16)
            eng.dma_start(pool_w, t["pool_w"].rearrange("g (k p) d -> p g k d", p=P)).then_inc(pool_w_in, 16)
            eng.wait_ge(small_in, SMALL)
            load_ffn(eng, 0)
            w = t["w_qkv"]
            for j in range(4):
                load_unit(eng, U_V + j, by_rows(w, 2 * j, 2, 2 * D, D))
            for h in range(HEADS):
                load_heads(eng, U_HEAD + h, w, h * VD, D + h * VD)
            for j in range(4):
                load_unit(eng, U_WO + j, by_rows(t["w_o"], 2 * j, 2, 0, D))
            load_ffn(eng, 1)
            w = t["w_in_2"]
            for j in range(2):
                load_unit(eng, U_QI + j, by_rows(w, 0, KT, O_QI + 256 * j, 256))
            load_unit(eng, U_KI, by_rows(w, 0, KT, O_KI, 72))
            for j in range(2):
                load_unit(eng, U_VA + j, by_rows(w, 4 * j, 4, O_VA, 512))
            for j in range(2):
                load_unit(eng, U_VB + j, by_rows(w, 4 * j, 4, O_VB, 512))
            for j in range(4):
                load_heads(eng, U_MOBA + j, w, O_QA + P * j, O_KA + P * j)
            for j in range(2):
                load_unit(eng, U_XC + j, by_rows(w, 0, KT, O_XC + 256 * j, 256))
            for j in range(4):
                load_heads(eng, U_DSA + j, w, O_QB + P * j, O_KB + P * j)
            for j in range(2):
                load_unit(eng, U_YC + j, by_rows(w, 0, KT, O_YC + 256 * j, 256))
            for c in range(6):
                of_half, b = CHUNKS[c]
                for j in range(2):
                    load_unit(eng, U_GATE + 3 * c + j, by_rows(w, 0, KT, O_GT + b * D + of_half * 512 + j * 256, 256))
                load_unit(eng, U_GATE + 3 * c + 2,
                          by_rows(t[("w_pa_2", "w_pb_2", "w_pc_2")[b]], 0, 4, of_half * 512, 512))
            for j in range(4):
                load_unit(eng, U_WO2 + j, by_rows(t["w_o_2"], 2 * j, 2, 0, D))
            load_mlp(eng)
            for i in range(NT):
                for h in range(2):
                    eng.wait_ge(out_ready, 2 * i + h + 1)
                    eng.dma_start(out[i * P:(i + 1) * P, half(h)], x[:, i, half(h)]).then_inc(stored, 16)
            eng.wait_ge(stored, 2 * 16 * NT)
            eng.wait_ge(vec_out, 16 * 8)

        def mm(*a, **k):
            return nc.tensor.matmul(*a, skip_group_check=True, **k)

        def three(out_, w, w_rest, a, a_rest, start, stop):
            mm(out_, w, a, start=start, stop=False)
            mm(out_, w, a_rest, start=False, stop=False)
            return mm(out_, w_rest, a, start=False, stop=stop)

        def project(slot, outs, hi, lo, nk=KT):
            whi, wlo = (part(w, slot, nk) for w in (w_hi, w_lo))
            for j, o in enumerate(outs):
                for k in range(nk):
                    c = slice(j * P, (j + 1) * P)
                    last = three(o, whi[:, k, c], wlo[:, k, c], hi[:, k, :], lo[:, k, :], k == 0, k == nk - 1)
            return last

        def first_project(eng, slot, rounds):
            whi, wlo = (part(w, slot, KT) for w in (w_hi, w_lo))
            for half in range(2):
                eng.wait_ge(x_ready, 2 * rounds + half + 1)
                for j, o in enumerate(two4):
                    for k in range(4 * half, 4 * half + 4):
                        c = slice(j * P, (j + 1) * P)
                        last = three(o, whi[:, k, c], wlo[:, k, c], x_hi[:, k, :], x_lo[:, k, :],
                                     (j, k) == (0, 0), k == KT - 1)
            return last

        def row_phase(eng, unit, rounds, begin=0):
            for j in range(begin, 2):
                eng.wait_ge(lo_done, unit + j + 1)
                if j == 0:
                    eng.wait_ge(x_ready, 2 * rounds + 1)
                rows((unit + j) % SLOTS, acc, x_hi, x_lo, 2 * j, 2, D, j == 0, False).then_inc(unit_done, 1)
            eng.wait_ge(lo_done, unit + 3)
            eng.wait_ge(x_ready, 2 * rounds + 2)
            last_pair(eng, unit + 2, (x_hi, x_lo, 4), (x_hi, x_lo, 6))

        def rows(slot, banks, hi, lo, k0, nk, width, first, final, tiles=range(NT)):
            whi, wlo = (part(w, slot, nk) for w in (w_hi, w_lo))
            for i in tiles:
                for k in range(nk):
                    a, al = (v[:, k0 + k, i * P:(i + 1) * P] for v in (hi, lo))
                    start, stop = first and k == 0, final and k == nk - 1
                    cols = [slice(n * 512, (n + 1) * 512) for n in range(width // 512)]
                    for n, c in enumerate(cols):
                        mm(banks[i][n], a, whi[:, k, c], start=start, stop=False)
                    for n, c in enumerate(cols):
                        mm(banks[i][n], a, wlo[:, k, c], start=False, stop=False)
                    for n, c in enumerate(cols):
                        last = mm(banks[i][n], al, whi[:, k, c], start=False, stop=stop)
            return last

        def last_pair(eng, unit, first, second, ready=None):
            whi, wlo = (part(w, (unit + 1) % SLOTS, 2) for w in (w_hi, w_lo))
            hi, lo, k0 = second
            for i in range(NT):
                last = rows(unit % SLOTS, acc, *first, 2, D, False, False, (i,))
                if i == 0:
                    eng.wait_ge(lo_done, unit + 2)
                    if ready:
                        ready()
                else:
                    last.then_inc(unit_done, 1)
                for n in range(2):
                    c, tok = half(n), slice(i * P, (i + 1) * P)
                    for k in range(2):
                        last = three(acc[i][n], hi[:, k0 + k, tok], lo[:, k0 + k, tok], whi[:, k, c], wlo[:, k, c],
                                     False, k == 1)
                    if (i, n) != (NT - 1, 1):
                        last.then_inc(rows_done, 1)
            last.then_inc(unit_done, 1)

        def quarter_done(eng, phase, units, i, h):
            if (i, h) == (NT - 1, 1):
                eng.wait_ge(unit_done, units)
            else:
                eng.wait_ge(rows_done, 3 * phase + 2 * i + h + 1)

        acc = [[bank[0][:, :], bank[1][:, :]], [bank[2][:, :], bank[3][:, :]]]
        two4 = [bank[4][:, 0:256], bank[4][:, 256:512]]
        two5 = [bank[5][:, 0:256], bank[5][:, 256:512]]

        def quarter(ev, i, h):
            if ev == O_NORM:
                return 4 * ev + 2 * h + i + 1, bank[5 + 2 * i if h else 7]
            return 4 * ev + 2 * i + h + 1, bank[4 + 2 * i + h]

        def pe_norm(eng, ev, src, quarters=((0, 0), (0, 1), (1, 0), (1, 1))):
            for i, h in quarters:
                count, b = quarter(ev, i, h)
                eng.wait_ge(n_ready, count)
                for k in range(4):
                    last = nc.tensor.transpose(b[:, k * P:(k + 1) * P],
                                               src[:, i, (4 * h + k) * P:(4 * h + k + 1) * P], ident[:, :])
                last.then_inc(n_turned, 1)

        def keep_warm(b, n):
            for _ in range(n):
                mm(b[:, 0:P], ident[:, :], ident[:, :], start=True, stop=True)

        def pe_norm_end(eng, ev, src, idle):
            pe_norm(eng, ev, src, ((0, 0), (0, 1)))
            keep_warm(bank[6], idle)
            pe_norm(eng, ev, src, ((1, 0), (1, 1)))
            keep_warm(bank[0], 9)

        def pe_ffn(eng, f, rounds):
            u0 = U_FFN[f]
            slots = [(u0 + 2 + j) % SLOTS for j in range(3)]

            def gate_up(i, unit):
                for j, banks in ((0, two4), (1, two5)):
                    eng.wait_ge(lo_done, unit + (j + 1))
                    eng.wait_ge((gate_read, up_read)[j], i + f * NCH)
                    project(slots[j], banks, x_hi, x_lo).then_inc(unit_done, 1)

            def down(i, unit, slot, first):
                eng.wait_ge(lo_done, unit + 1)
                eng.wait_ge(h_ready, i + (f * NCH + 1))
                rows(slot, acc, h_hi[0], h_lo[0], 0, 2, D, first, False).then_inc(unit_done, 1)

            eng.wait_ge(lo_done, u0 + 1)
            first_project(eng, u0 % SLOTS, rounds).then_inc(unit_done, 1)
            eng.wait_ge(lo_done, u0 + 2)
            project((u0 + 1) % SLOTS, two5, x_hi, x_lo).then_inc(unit_done, 1)
            gate_up(1, u0 + 2)
            down(0, u0 + 4, slots[2], True)
            with eng.Fori(2, NCH - 1) as i:
                unit = i * 3 + (u0 - 1)
                gate_up(i, unit)
                down(i - 1, unit + 2, slots[2], False)
            end = u0 + 3 * NCH
            gate_up(NCH - 1, end - 4)
            eng.wait_ge(lo_done, end - 1)
            eng.wait_ge(h_ready, (f + 1) * NCH - 1)
            last_pair(eng, end - 2, (h_hi[0], h_lo[0], 0), (h_hi[1], h_lo[1], 0),
                      lambda: eng.wait_ge(h_ready, (f + 1) * NCH))

        def pe_mlp(eng):
            def up(i, unit, slot):
                eng.wait_ge(lo_done, unit + 1)
                eng.wait_ge(sq_done, i)
                project(slot, two4, x_hi, x_lo).then_inc(unit_done, 1)

            def down(i, unit, slot, first):
                eng.wait_ge(lo_done, unit + 1)
                eng.wait_ge(m_ready, i + 1)
                rows(slot, acc, h_hi[0], h_lo[0], 0, 2, D, first, False).then_inc(unit_done, 1)

            eng.wait_ge(lo_done, U_MLP + 1)
            first_project(eng, U_MLP % SLOTS, 6).then_inc(unit_done, 1)
            for j in range(3):
                unit = U_MLP + 1 + 2 * j
                up(j + 1, unit, unit % SLOTS)
                down(j, unit + 1, (unit + 1) % SLOTS, j == 0)
            with eng.Fori(1, (NCH2 - 1) // 3 - 1) as i:
                for j in range(3):
                    unit = i * 6 + (U_MLP + 1 + 2 * j)
                    up(i * 3 + (j + 1), unit, (U_MLP + 1 + 2 * j) % SLOTS)
                    down(i * 3 + j, unit + 1, (U_MLP + 2 + 2 * j) % SLOTS, False)
            for c in range(NCH2 - 3, NCH2):
                unit = U_MLP + 2 * c - 1
                up(c, unit, unit % SLOTS)
                if c < NCH2 - 1:
                    down(c - 1, unit + 1, (unit + 1) % SLOTS, False)
            eng.wait_ge(lo_done, U_END - 1)
            eng.wait_ge(m_ready, NCH2 - 1)
            last_pair(eng, U_END - 2, (h_hi[0], h_lo[0], 0), (h_hi[1], h_lo[1], 0),
                      lambda: eng.wait_ge(m_ready, NCH2))

        def proj_out(unit):
            return two5 if unit in BANK5 else two4

        def project_free(eng, unit):
            before = COPIED[unit] - (unit - 1 in BANK5)
            if before and unit not in BANK5:
                eng.wait_ge(proj_copied, before)

        def pe_turn_probs(eng, a):
            eng.wait_ge(prob_ready, a + 1)
            if 1 <= a <= A_MOBA:
                eng.wait_ge(pt_copied, a)
            elif a > A_MOBA:
                eng.wait_ge(pt_copied2, a - A_MOBA)
            for m in range(1 if a < A_MOBA else 2):
                for b in range(3):
                    c = slice(b * P, (b + 1) * P)
                    last = nc.tensor.transpose(bank[6 + m][:, c], prob[:, m, c], ident[:, :])
            last.then_inc(turned, 1)

        def pe_score(eng, a, unit):
            eng.wait_ge(proj_copied, COPIED[unit] + 1)
            if a >= 2:
                eng.wait_ge(logits_read, a - 1)
            q_k = qk[a % 2]
            for m in range(2):
                s, r = bank[2 * (a % 2) + m], slice(m * DH, (m + 1) * DH)
                mm(s[:, 0:P], q_k[r, 0, 0:P], q_k[r, 1, 0:P], start=True, stop=True)
                last = mm(s[:, P:384], q_k[r, 0, P:SEQ], q_k[r, 1, 0:SEQ], start=True, stop=True)
            last.then_inc(scored, 1)

        def pe_apply(eng, a):
            if a < A_MOBA:
                eng.wait_ge(pt_copied, a + 1)
            else:
                eng.wait_ge(pt_copied2, a - A_MOBA + 1)
            if a >= 1:
                eng.wait_ge(o_copied, a)
            if a < A_MOBA:
                h = slice(a * VD, (a + 1) * VD)
                mm(bank[5][:, 0:P], prob_t[:, 0, 0:P], v1[:, 0, h], start=True, stop=True)
                mm(bank[5][:, P:SEQ], prob_t[:, 0, P:SEQ], v1[:, 0, h], start=True, stop=False)
                last = mm(bank[5][:, P:SEQ], prob_t[:, 0, SEQ:384], v1[:, 1, h], start=False, stop=True)
            else:
                v = v_a if a < A_DSA else v_b
                for m in range(2):
                    hd = 2 * ((a - A_MOBA) % 4) + m
                    o, h = bank[5][m * DH:(m + 1) * DH, :], slice(hd * DH, (hd + 1) * DH)
                    mm(o[:, 0:SEQ], v[:, 0, h], prob_t[:, m, 0:SEQ], start=True, stop=False)
                    last = mm(o[:, P:SEQ], v[:, 1, h], prob_t[:, m, SEQ:384], start=False, stop=True)
            last.then_inc(applied, 1)

        def pe_dots(eng, g):
            if g >= 1:
                eng.wait_ge(dots_relu, 2 * g)
            for m in range(2):
                r, s = slice(m * DH, (m + 1) * DH), bank[2 + m]
                mm(s[:, 0:P], qi[r, g, 0:P], ki[r, 0:P], start=True, stop=True)
                last = mm(s[:, P:384], qi[r, g, P:SEQ], ki[r, 0:SEQ], start=True, stop=True)
            last.then_inc(dotted, 1)

        def pe_mixer(eng):
            score_unit = {step_of(u): u for u in range(U_QI, U_GATE)}
            for unit, apply, score_step in TURNS:
                if apply is not None:
                    pe_turn_probs(eng, apply)
                if score_step is not None:
                    pe_score(eng, score_step, score_unit[score_step])
                eng.wait_ge(lo_done, unit + 1)
                s = unit % SLOTS
                if unit in COPIED:
                    project_free(eng, unit)
                if unit == U_KI:
                    whi, wlo = (part(w, s, KT) for w in (w_hi, w_lo))
                    for k in range(KT):
                        three(bank[4][:, 0:SEQ], whi[:, k, 0:P], wlo[:, k, 0:P], x_hi[:, k, :], x_lo[:, k, :],
                              k == 0, k == KT - 1)
                    c = slice(P, P + IDX_HEADS)
                    for k in range(KT):
                        last = three(bank[4][0:IDX_HEADS, SEQ:2 * SEQ], whi[:, k, c], wlo[:, k, c], x_hi[:, k, :],
                                     x_lo[:, k, :], k == 0, k == KT - 1)
                elif U_VA <= unit < U_MOBA:
                    j = (unit - U_VA) % 2
                    if unit == U_VB:
                        eng.wait_ge(v_copied, 2)
                    last = rows(s, [[bank[0][:, :]], [bank[1][:, :]]], x_hi, x_lo, 4 * j, 4, 512, j == 0, j == 1)
                elif unit == U_QI:
                    last = first_project(eng, s, 4)
                else:
                    last = project(s, proj_out(unit), x_hi, x_lo)
                last.then_inc(unit_done, 1)
                if U_VA <= unit < U_MOBA:
                    if unit == U_VA:
                        eng.wait_ge(proj_copied, COPIED[U_KI] + 1)
                        for i in range(NT):
                            last = nc.tensor.transpose(bank[5][:, IDX_HEADS * i:IDX_HEADS * (i + 1)],
                                                       wi_t[:, i * P:(i + 1) * P], ident[0:IDX_HEADS, 0:IDX_HEADS])
                        last.then_inc(wi_turned, 1)
                    pe_dots(eng, unit - U_VA)
                if unit == U_VB + 1:
                    eng.wait_ge(v_copied, 3)
                    eng.wait_ge(dots_relu, 8)
                if apply is not None:
                    pe_apply(eng, apply)

        def pe_gates(eng):
            eng.wait_ge(conv_ready, CT)
            eng.wait_ge(wri_in, 64)
            eng.wait_ge(logits_read, A_END)
            for m in range(2):
                for c in range(CT):
                    last = mm(bank[2 * m + c // 2][:, (c % 2) * 256:(c % 2) * 256 + 256], wri[:, m, c, :],
                              conv[:, c, :], start=True, stop=True)
            last.then_inc(ri_ready, 1)
            eng.wait_ge(proj_copied, len(COPIED))
            eng.wait_ge(o_copied, A_END)
            eng.wait_ge(o_squared, A_END)
            eng.wait_ge(pt_copied2, A_END - A_MOBA)
            for c in range(6):
                for j, banks in ((0, two4), (1, two5)):
                    unit = U_GATE + 3 * c + j
                    eng.wait_ge(lo_done, unit + 1)
                    if c:
                        eng.wait_ge(gate_act, 2 * c + j - 1)
                    project(unit % SLOTS, banks, x_hi, x_lo).then_inc(unit_done, 1)
                unit = U_GATE + 3 * c + 2
                eng.wait_ge(lo_done, unit + 1)
                if c:
                    eng.wait_ge(p_read, c)
                if c == 4:
                    eng.wait_ge(y_ready, 1)
                b = CHUNKS[c][1]
                project(unit % SLOTS, [bank[6 + j // 2][:, (j % 2) * 256:(j % 2) * 256 + 256] for j in range(4)],
                        y_hi[:, b], y_lo[:, b], nk=4).then_inc(unit_done, 1)

        @block.tensor
        def _(eng):
            eng.wait_ge(set_done, 2)
            for _ in range(20):
                mm(bank[7][:, 0:P], ones, ones, start=True, stop=True)
            eng.wait_ge(pool_m_in, 16)
            for i, (src, dst) in enumerate(((slice(0, P + REACH), 0), (slice(P + REACH, 2 * P + REACH), P))):
                eng.wait_ge(x_in[i], 16)
                for k in range(KT):
                    b, o, g = bank[k // 2], (k % 2) * 256, k // 2
                    last = mm(b[:, o + dst:o + dst + src.stop - src.start], x[:, i, k * P:(k + 1) * P],
                              pool_m[:, g, src], start=(i == 0 and k % 2 == 0), stop=(i == 1))
                    if i and k % 2:
                        last.then_inc(pooled, 1)
            eng.wait_ge(small_in, SMALL)
            nc.tensor.transpose(bank[4][:, 0:NROWS], prow, ident[0:NROWS, 0:NROWS]).then_inc(pe_start, 1)
            mm(bank[5][0:24, 0:384], tab, onehot, start=True, stop=True).then_inc(pe_start, 1)
            eng.wait_ge(v_start, 1)
            mm(bank[6][:, 0:2], ones, lprod, start=True, stop=True).then_inc(pe_start, 1)
            eng.wait_ge(pool_scaled, 1)
            eng.wait_ge(pool_copied, NG)
            for i in range(NT):
                for g in range(NG):
                    for k in range(2):
                        last = mm(acc[i][g // 2][:, (g % 2) * 256:(g % 2) * 256 + 256],
                                  pool_d[:, 2 * g + k, i * P:(i + 1) * P], pool_w[:, g, k, :],
                                  start=(k == 0), stop=(k == 1))
                    if g % 2:
                        last.then_inc(mixed, 1)
            eng.wait_ge(v_start, 4)
            eng.wait_ge(s_start, 1)
            pe_norm_end(eng, 0, x, 1)
            pe_ffn(eng, 0, 0)
            pe_norm(eng, V_NORM, x, ((0, 0), (0, 1)))
            keep_warm(bank[6], 14)
            eng.wait_ge(lo_done, U_V + 1)
            eng.wait_ge(x0_ready, 1)
            rows(U_V % SLOTS, acc, x_hi, x_lo, 0, 2, D, True, False, (0,))
            pe_norm(eng, V_NORM, x, ((1, 0), (1, 1)))
            eng.wait_ge(lo_done, U_V + 2)
            rows((U_V + 1) % SLOTS, acc, x_hi, x_lo, 2, 2, D, False, False, (0,))
            eng.wait_ge(x_ready, 2 * V_NORM + 1)
            for j in range(2):
                rows((U_V + j) % SLOTS, acc, x_hi, x_lo, 2 * j, 2, D, j == 0, False, (1,)).then_inc(unit_done, 1)
            for j in (2, 3):
                eng.wait_ge(lo_done, U_V + j + 1)
                eng.wait_ge(x_ready, 2 * V_NORM + 2)
                rows((U_V + j) % SLOTS, acc, x_hi, x_lo, 2 * j, 2, D, j == 0, j == 3).then_inc(unit_done, 1)
            for unit, apply, score_step in HEAD_TURNS[:-1]:
                if apply is not None:
                    pe_turn_probs(eng, apply)
                if score_step is not None:
                    if score_step == 0:
                        eng.wait_ge(v_copied, 1)
                    pe_score(eng, score_step, U_HEAD + score_step)
                if unit is not None:
                    eng.wait_ge(lo_done, unit + 1)
                    project_free(eng, unit)
                    project(unit % SLOTS, proj_out(unit), x_hi, x_lo).then_inc(unit_done, 1)
                if apply is not None:
                    pe_apply(eng, apply)
                if unit == U_HEAD + 6:
                    pe_norm(eng, O_NORM, o1, ((0, 0),))
                if unit == U_HEAD + 7:
                    eng.wait_ge(xf0_ready, 2 * O_NORM + 1)
                    pe_norm(eng, O_NORM, o1, ((1, 0),))
            eng.wait_ge(lo_done, U_WO + 1)
            eng.wait_ge(x_ready, 2 * O_NORM + 1)
            eng.wait_ge(logits_read, HEADS - 1)
            rows(U_WO % SLOTS, acc, x_hi, x_lo, 0, 2, D, True, False, (0,))
            eng.wait_ge(logits_read, HEADS)
            rows(U_WO % SLOTS, acc, x_hi, x_lo, 0, 2, D, True, False, (1,)).then_inc(unit_done, 1)
            pe_turn_probs(eng, HEADS - 1)
            pe_apply(eng, HEADS - 1)
            eng.wait_ge(lo_done, U_WO + 2)
            rows((U_WO + 1) % SLOTS, acc, x_hi, x_lo, 2, 2, D, False, False).then_inc(unit_done, 1)
            eng.wait_ge(o_copied, HEADS)
            pe_norm(eng, O_NORM, o1, ((0, 1), (1, 1)))
            eng.wait_ge(proj_copied, HEADS)
            keep_warm(bank[4], 16)
            row_phase(eng, U_WO, 2, 2)
            pe_norm_end(eng, 3, x, 10)
            pe_ffn(eng, 1, 3)
            keep_warm(bank[4], 30)
            pe_norm_end(eng, 4, nbuf, 1)
            pe_mixer(eng)
            pe_gates(eng)
            row_phase(eng, U_WO2, 5)
            pe_norm_end(eng, 5, nbuf, 10)
            pe_mlp(eng)

        def split_views(slot, indexer):
            if indexer:
                r = raw[slot][:, 0:72 * KT].rearrange("p (k c) -> p k c", k=KT)
                return [[(o[:, :, 0:64], r[:, :, 0:64]), (o[:, :, 64:128], r[:, :, 0:64]),
                         (o[:, :, 128:136], r[:, :, 64:72])] for o in (part(w, slot, KT) for w in (w_hi, w_lo))]
            return [[(w[slot][:, :], raw[slot][:, :])] for w in (w_hi, w_lo)]

        def round_unit(eng, unit, slot, landed, fresh=False, indexer=False):
            eng.wait_ge(raw_in[slot], landed)
            if not fresh:
                eng.wait_ge(unit_done, unit - (SLOTS - 1))
            for o, i in split_views(slot, indexer)[0]:
                last = nc.scalar.activation(o, i, ACT.Copy)
            last.then_inc(hi_done, 1)

        def rest_unit(eng, unit, slot, indexer=False):
            eng.wait_ge(hi_done, unit + 1)
            his, los = split_views(slot, indexer)
            for (h, _), (o, i) in zip(his, los):
                last = nc.vector.tensor_tensor(o, i, h.bitcast(F32), ALU.subtract)
            last.then_inc(lo_done, 1)

        def s_split(eng, unit):
            if unit < U_END:
                round_unit(eng, unit, unit % SLOTS, 32 * (unit // SLOTS + 1), unit < SLOTS, unit == U_KI)

        def v_split(eng, unit):
            if unit < U_END:
                rest_unit(eng, unit, unit % SLOTS, unit == U_KI)

        def s_transposed(eng, ev, h, gain, offset):
            count, b = quarter(ev, 0, h)
            eng.wait_ge(n_turned, count)
            if ev == O_NORM:
                last = nc.scalar.activation(xf[:, 4 * h:4 * h + 4, 0:P], b[:, :].rearrange("p (k t) -> p k t", k=4),
                                            ACT.Identity, scale=gain(0))
                last.then_inc(xf0_ready, 1)
                return
            for k in range(4 * h, 4 * h + 4):
                more = {"bias": offset(k)} if offset else {}
                last = nc.scalar.activation(xf[:, k, 0:P], b[:, (k % 4) * P:(k % 4 + 1) * P], ACT.Identity,
                                            scale=gain(k), **more)
            last.then_inc(xf0_ready, 1)

        def s_high(eng, ev, i, h):
            eng.wait_ge((xf0_ready, xf1_ready)[i], 2 * ev + h + 1)
            q = slice(i * P, (i + 1) * P)
            nc.scalar.activation(x_hi[:, 4 * h:4 * h + 4, q], xf[:, 4 * h:4 * h + 4, q],
                                 ACT.Copy).then_inc(x_rounded, 1)

        def s_norm_split(eng, ev, units, gain, offset):
            for h in range(2):
                s_transposed(eng, ev, h, gain, offset)
                if units:
                    eng.wait_ge(unit_done, units)
                s_high(eng, ev, 0, h)
            for h in range(2):
                s_high(eng, ev, 1, h)

        hidden_rows = ffn_h.rearrange("p (a b) -> p a b", a=2)

        def s_ffn(eng, f):
            u0 = U_FFN[f]

            def tanh_of(unit):
                eng.wait_ge(unit_done, unit + 1)
                nc.scalar.activation(ffn_e, bank[4][:, :], ACT.Tanh, scale=0.5).then_inc(tanh_done, 1)

            def round_h(i, before, buf=0):
                eng.wait_ge(up_read, i + (f * NCH + 1))
                if before is not None:
                    eng.wait_ge(unit_done, before)
                nc.scalar.activation(h_hi[buf], hidden_rows, ACT.Copy).then_inc(h_rounded, 1)

            s_split(eng, u0 + 2)
            tanh_of(u0)
            s_split(eng, u0 + 3)
            round_h(0, None)
            with eng.Fori(1, NCH - 1) as i:
                unit = i * 3 + (u0 - 1)
                for j in range(3):
                    nxt = u0 + 4 + j
                    round_unit(eng, unit + 2 + j, nxt % SLOTS, i * 32 + (nxt // SLOTS) * 32)
                    if j == 0:
                        tanh_of(unit)
                round_h(i, unit + 3)
            unit = u0 + 3 * NCH - 4
            s_split(eng, unit + 2)
            tanh_of(unit)
            s_split(eng, unit + 3)
            round_h(NCH - 1, None, 1)
            s_split(eng, unit + 4)
            s_split(eng, u0 + 3 * NCH + 1)

        def s_mlp(eng):
            def relu_of(unit):
                eng.wait_ge(unit_done, unit + 1)
                nc.scalar.activation(ffn_e, bank[4][:, :], ACT.Relu).then_inc(relu_done, 1)

            def round_h(i, before, buf=0):
                eng.wait_ge(sq_done, i + 1)
                if before is not None:
                    eng.wait_ge(unit_done, before)
                nc.scalar.activation(h_hi[buf], hidden_rows, ACT.Copy).then_inc(m_rounded, 1)

            s_split(eng, U_MLP + 2)
            relu_of(U_MLP)
            round_h(0, None)
            with eng.Fori(0, (NCH2 - 1) // 3 - 1) as i:
                for j in range(3):
                    unit = i * 6 + (U_MLP + 1 + 2 * j)
                    nxt = U_MLP + 3 + 2 * j
                    round_unit(eng, unit + 2, nxt % SLOTS, i * 64 + 32 * (nxt // SLOTS + 1))
                    relu_of(unit)
                    round_unit(eng, unit + 3, (nxt + 1) % SLOTS, i * 64 + 32 * ((nxt + 1) // SLOTS + 1))
                    round_h(i * 3 + (j + 1), unit + 2)
            for c in range(NCH2 - 3, NCH2):
                unit = U_MLP + 2 * c - 1
                s_split(eng, unit + 2)
                relu_of(unit)
                s_split(eng, unit + 3)
                if c < NCH2 - 1:
                    round_h(c, unit + 2)
                else:
                    round_h(c, None, 1)

        def s_softmax(eng, a):
            eng.wait_ge(logits_read, a + 1)
            if a:
                eng.wait_ge(prob_ready, a)
            for m in range(2):
                for i, c in enumerate((slice(0, P), slice(P, 384))):
                    last = nc.scalar.activation(prob_e[:, m, c], logit[:, m, c], ACT.Exp, scale=-1.0,
                                                bias=nmax[:, m, i:i + 1], accum_out=zsum[:, m, i:i + 1])
            last.then_inc(exp_ready, 1)

        def s_out_step(eng, a):
            if a < A_MOBA:
                eng.wait_ge(o_copied, a + 1)
                if a:
                    eng.wait_ge(o_squared, a)
                for i in range(NT):
                    last = nc.scalar.activation(head_scr[:, i, :], o1[:, i, a * VD:(a + 1) * VD], ACT.Square,
                                                accum_out=sumsq[:, i, a:a + 1])
            else:
                eng.wait_ge(applied, a + 1)
                b, pr = (a - A_MOBA) // 4, (a - A_MOBA) % 4
                last = nc.scalar.activation(y_hi[:, b, pr, :], bank[5][:, 0:SEQ], ACT.Copy)
            last.then_inc(o_squared, 1)

        def s_copy_unit(eng, unit):
            eng.wait_ge(unit_done, unit + 1)
            both = bank[5 if unit in BANK5 else 4][:, :].rearrange("p (a b) -> p a b", a=2)
            if unit == U_KI:
                nc.scalar.activation(wi_t[:, :], bank[4][0:IDX_HEADS, SEQ:2 * SEQ], ACT.Copy)
                nc.scalar.activation(ki, bank[4][:, 0:SEQ], ACT.Copy).then_inc(proj_copied, 1)
                return
            if step_of(unit) is not None:
                dst = qk[step_of(unit) % 2]
            elif unit < U_KI:
                dst = qi[:, 2 * (unit - U_QI):2 * (unit - U_QI) + 2, :]
            elif unit < U_DSA:
                dst = xc[:, 2 * (unit - U_XC):2 * (unit - U_XC) + 2, 3:259]
            else:
                dst = yc[:, 2 * (unit - U_YC):2 * (unit - U_YC) + 2, :]
            nc.scalar.activation(dst, both, ACT.Copy).then_inc(proj_copied, 1)

        def s_dots(eng, g):
            if g == 0:
                eng.wait_ge(wi_turned, 1)
                nc.scalar.activation(wi_s[:, :, :],
                                     bank[5][:, 0:NT * IDX_HEADS].rearrange("p (a b) -> p a b", a=NT), ACT.Copy)
            eng.wait_ge(dotted, g + 1)
            for m in range(2):
                if g:
                    eng.wait_ge(dots_used, 2 * g + m - 1)
                nc.scalar.activation(dots[:, m, :], bank[2 + m][:, 0:384], ACT.Relu).then_inc(dots_relu, 1)

        def s_mixer(eng):
            for unit, apply, score_step in TURNS:
                if apply is not None:
                    eng.wait_ge(turned, apply + 1)
                    if apply > A_MOBA:
                        eng.wait_ge(applied, apply)
                    for m in range(2):
                        last = nc.scalar.activation(prob_t[:, m, :], bank[6 + m][:, 0:384], ACT.Copy)
                    last.then_inc(pt_copied2, 1)
                s_split(eng, unit + 2)
                if score_step is not None:
                    s_softmax(eng, score_step)
                if unit in COPIED:
                    s_copy_unit(eng, unit)
                if unit in (U_VA + 1, U_VB + 1):
                    eng.wait_ge(unit_done, unit + 1)
                    v = v_a if unit < U_VB else v_b
                    for i in range(NT):
                        last = nc.scalar.activation(v[:, i, :], bank[i][:, :], ACT.Copy)
                    last.then_inc(v_copied, 1)
                if U_VA <= unit < U_MOBA:
                    s_dots(eng, unit - U_VA)
                if apply is not None:
                    s_out_step(eng, apply)

        def s_merged(eng, h):
            eng.wait_ge(merged_ready, h + 1)
            nc.scalar.activation(x_hi[:, 4 * h:4 * h + 4, :], merged[:, 4 * h:4 * h + 4, :],
                                 ACT.Identity, scale=0.5).then_inc(merged_rounded, 1)

        def s_gates(eng):
            for c in range(6):
                for j in range(3):
                    s_split(eng, U_GATE + 3 * c + j + 2)
                    if (c, j) == (0, 0):
                        eng.wait_ge(ri_ready, 1)
                        for m, o, f, k in ((0, gr, ACT.Exp, -1.0), (1, gi, ACT.Tanh, 0.5)):
                            for n in range(CT):
                                src = bank[2 * m + n // 2][:, (n % 2) * 256:(n % 2) * 256 + 256]
                                last = nc.scalar.activation(o[:, n, :], src, f, scale=k,
                                                            bias=gate_b[:, 4 * m + n:4 * m + n + 1])
                            last.then_inc(ri_act, 1)
                        eng.wait_ge(proj_copied, len(COPIED))
                        nc.scalar.activation(gl, yc, ACT.Square).then_inc(gelu_sq, 1)
                    if (c, j) == (1, 2):
                        eng.wait_ge(ri_sig, CT)
                        for n in range(CT):
                            nc.scalar.activation(rt[:, n, :], gr[:, n, :], ACT.Tanh, scale=lru_c[:, n:n + 1])
                            nc.scalar.activation(ra[:, n, :], gr[:, n, :], ACT.Exp, scale=lru_c[:, n:n + 1])
                            last = nc.scalar.activation(rq[:, n, :], gr[:, n, :], ACT.Exp,
                                                        scale=lru_c[:, CT + n:CT + n + 1])
                        last.then_inc(lru_act, 1)
                        eng.wait_ge(gelu_z, 1)
                        nc.scalar.activation(gl, gl, ACT.Tanh, scale=GELU_B).then_inc(gelu_t, 1)
                    if (c, j) == (2, 2):
                        eng.wait_ge(lru_u2, 1)
                        nc.scalar.activation(rt, rt, ACT.Sqrt, scale=-0.25).then_inc(lru_root, 1)
                    if (c, j) == (4, 0):
                        eng.wait_ge(yc_ready, 1)
                        nc.scalar.activation(y_hi[:, 2], yc, ACT.Copy).then_inc(yc_rounded, 1)
                    if (c, j) == (5, 2):
                        eng.wait_ge(unit_done, U_WO2 - 1)
                        s_merged(eng, 0)
                    if j < 2:
                        eng.wait_ge(unit_done, U_GATE + 3 * c + j + 1)
                        if c:
                            eng.wait_ge(p_read, c)
                        nc.scalar.activation(sig[:, 2 * j:2 * j + 2, :],
                                             bank[4 + j][:, :].rearrange("p (a b) -> p a b", a=2),
                                             ACT.Tanh, scale=0.5).then_inc(gate_act, 1)

            s_merged(eng, 1)

        def s_rms(eng, n, tiles=range(NT)):
            for i in tiles:
                for h in range(2):
                    eng.wait_ge(z_ready, 4 * n + 2 * i + h + 1)
                    c = slice(h * 512, (h + 1) * 512)
                    nc.scalar.activation(sq_scr[:, i, c], x[:, i, c], ACT.Square,
                                         accum_out=sumsq[:, i, h:h + 1]).then_inc(ss_ready, 1)

        @block.scalar
        def _(eng):
            for name, (row, n) in ROWS.items():
                eng.dma_start(prow[row:row + n, :], t[name]).then_inc(small_in, 16)
            for dst, src in ((onehot, t["c_onehot"]), (vecmask, t["c_vecmask"]), (ident[:, :], t["c_ident"]),
                             (causal[:, :], t["c_causal"]), (tab[:, 0:8], t["rel_table"]),
                             (tab[:, 8:24], t["rel_bias_2"])):
                eng.dma_start(dst, src).then_inc(small_in, 16)
            with nc.allow_non_contiguous_dma("256 numbers"):
                eng.dma_start(lp, t["lam_p"].rearrange("a b -> b a")).then_inc(small_in, 16)
            for g in range(NG):
                eng.wait_ge(pooled, g + 1)
                nc.scalar.activation(pool_d[:, 2 * g:2 * g + 2, :], bank[g][:, :].rearrange("p (a b) -> p a b", a=2),
                                     ACT.Copy).then_inc(pool_copied, 1)
            s_split(eng, 0)
            eng.wait_ge(v_start, 3)
            nc.scalar.activation(sp[:, 2, :], sp[:, 1, :], ACT.Exp, scale=-1.0).then_inc(s_link, 1)
            eng.wait_ge(pe_start, 3)
            nc.scalar.activation(e_lam[:, :], bank[6][:, 0:2], ACT.Exp).then_inc(s_start, 1)
            s_split(eng, 1)
            eng.wait_ge(s_link, 1)
            nc.scalar.activation(sp[:, 3, :], sp[:, 2, :], ACT.Ln, bias=1.0).then_inc(s_start, 1)
            s_norm_split(eng, 0, None, lambda k: col("ln_mix_g", k), lambda k: col("ln_mix_b", k))
            s_ffn(eng, 0)
            s_norm_split(eng, 1, U_V, lambda k: col("ln_ffn_g", k), lambda k: col("ln_ffn_b", k))
            for j in range(4):
                s_split(eng, U_V + j + 2)
            eng.wait_ge(unit_done, U_V + 4)
            for i in range(NT):
                for h in range(2):
                    last = nc.scalar.activation(v1[:, i, h * 512:(h + 1) * 512], acc[i][h], ACT.Copy)
            last.then_inc(v_copied, 1)
            out_gain = lambda k: sub_gain[:, 0:1]
            for unit, apply, score_step in HEAD_TURNS[:-2]:
                if unit == U_HEAD + 7:
                    s_transposed(eng, O_NORM, 0, out_gain, None)
                s_split(eng, unit + 2)
                if score_step is not None:
                    s_softmax(eng, score_step)
                s_copy_unit(eng, unit)
                if apply is not None:
                    s_out_step(eng, apply)
            for i in range(NT):
                s_high(eng, O_NORM, i, 0)
            s_softmax(eng, HEADS - 1)
            s_out_step(eng, HEADS - 2)
            s_split(eng, U_WO + 2)
            s_out_step(eng, HEADS - 1)
            s_split(eng, U_WO + 3)
            s_transposed(eng, O_NORM, 1, out_gain, None)
            for i in range(NT):
                s_high(eng, O_NORM, i, 1)
            s_split(eng, U_WO + 4)
            s_split(eng, U_WO + 5)
            s_norm_split(eng, 3, U_FFN[1], lambda k: col("ln_mix_g", 8 + k), lambda k: col("ln_mix_b", 8 + k))
            s_ffn(eng, 1)
            s_rms(eng, 0)
            s_norm_split(eng, 4, U_QI, lambda k: col("norm_mix_g_2", k), None)
            s_mixer(eng)
            s_gates(eng)
            for j in range(3):
                s_split(eng, U_WO2 + j + 2)
            s_rms(eng, 1, (0,))
            s_split(eng, U_MLP + 1)
            s_rms(eng, 1, (1,))
            s_norm_split(eng, 5, U_MLP, lambda k: col("norm_mlp_g_2", k), None)
            s_mlp(eng)
            s_rms(eng, 2)

        class Link:

            def __init__(self, eng, s):
                self.eng, self.s, self.n = eng, s, 0

            def __call__(self, ins):
                self.n += 1
                ins.then_inc(self.s, 1)
                self.eng.wait_ge(self.s, self.n)

        V = nc.vector
        TILE_COLS = (slice(0, P), slice(P, 384))
        TABLE_COLS = (slice(P, SEQ), slice(0, SEQ))
        var_count = [0]

        def variance(out_cols, src, factor, eps):
            V.tensor_scalar(vareps[:, out_cols], src, factor, eps, ALU.mult, ALU.add).then_inc(var_ready, 1)
            var_count[0] += 1
            return var_count[0]

        def v_layernorm(eng, link, residual, centred=None, meanwhile=None, together=False):
            first = None
            for i in range(NT):
                for h in range(2):
                    residual(i, h)
                    ins = V.bn_stats(stats[:, i, h, :], x[:, i, half(h)])
                link(ins)
                link(V.bn_aggr(mv[:, i, :], stats[:, i, :, :]))
                n = variance(slice(i, i + 1), mv[:, i, 1:2], 1.0, LN_EPS)
                if centred:
                    centred(i)
                if meanwhile and i:
                    meanwhile()
                if together and i == 0:
                    first = n
                    continue
                if first:
                    eng.wait_ge(rstd_ready, first)
                    yield 0
                eng.wait_ge(rstd_ready, n)
                yield i

        def v_tile1(eng, ev, h, gain, offset=None):
            count, b = quarter(ev, 1, h)
            eng.wait_ge(n_turned, count)
            if offset:
                for k in range(4 * h, 4 * h + 4):
                    last = V.tensor_scalar(xf[:, k, P:SEQ], b[:, (k % 4) * P:(k % 4 + 1) * P], gain(k), offset(k),
                                           ALU.mult, ALU.add)
            else:
                last = V.tensor_tensor(xf[:, 4 * h:4 * h + 4, P:SEQ], b[:, :].rearrange("p (k t) -> p k t", k=4),
                                       gain(h).unsqueeze(2).broadcast_to([P, 4, P]), ALU.mult)
            last.then_inc(xf1_ready, 1)

        def v_low(eng, ev, i, h):
            eng.wait_ge(x_rounded, quarter(ev, i, h)[0])
            k, q = slice(4 * h, 4 * h + 4), slice(i * P, (i + 1) * P)
            ins = V.tensor_tensor(x_lo[:, k, q], xf[:, k, q], x_hi[:, k, q].bitcast(F32), ALU.subtract)
            if i:
                ins.then_inc(x_ready, 1)
            elif (ev, h) == (V_NORM, 0):
                ins.then_inc(x0_ready, 1)

        def v_transposed(eng, ev, unit, gain, offset=None):
            if ev == V_NORM:
                v_split(eng, unit)
                v_tile1(eng, ev, 0, gain, offset)
                v_low(eng, ev, 1, 0)
                v_low(eng, ev, 0, 1)
                v_tile1(eng, ev, 1, gain, offset)
                v_low(eng, ev, 1, 1)
                return
            for h in range(2):
                v_low(eng, ev, 0, h)
                v_tile1(eng, ev, h, gain, offset)
                v_low(eng, ev, 1, h)
            v_split(eng, unit)

        def v_merged_low(eng, h):
            eng.wait_ge(merged_rounded, h + 1)
            k = slice(4 * h, 4 * h + 4)
            V.scalar_tensor_tensor(x_lo[:, k, :], merged[:, k, :], 0.5, x_hi[:, k, :].bitcast(F32),
                                   ALU.mult, ALU.subtract).then_inc(x_ready, 1)

        def v_residual(eng, phase, units, i, h, factor):
            quarter_done(eng, phase, units, i, h)
            c = half(h)
            return V.scalar_tensor_tensor(x[:, i, c], x[:, i, c], factor, acc[i][h], ALU.mult, ALU.add)

        def v_ln_phase(eng, link, ev, phase, unit, nat, g, b, layer):
            eng.wait_ge(nat_ready, nat)
            begin = (lambda: v_low(eng, ev, 0, 0)) if ev == V_NORM else None
            for i in v_layernorm(eng, link, lambda i, h: link(v_residual(eng, phase, unit + 1, i, h, ALPHA)),
                                 meanwhile=begin):
                v_normalise(i)
            v_transposed(eng, ev, unit + 2, lambda k: col(g, 8 * layer + k), lambda k: col(b, 8 * layer + k))

        def v_normalise(i):
            for h in range(2):
                V.tensor_scalar(x[:, i, half(h)], x[:, i, half(h)], mv[:, i, 0:1], rstd[:, i:i + 1],
                                ALU.subtract, ALU.mult).then_inc(n_ready, 1)

        def rms_variance(eng, link, n_rms, i):
            eng.wait_ge(ss_ready, 4 * n_rms + 2 * i + 2)
            link(V.tensor_tensor(sumsq[:, i, 2:3], sumsq[:, i, 0:1], sumsq[:, i, 1:2], ALU.add))
            return variance(slice(i, i + 1), sumsq[:, i, 2:3], 1.0 / D, EPS)

        def v_rms_rows(eng, i, n):
            eng.wait_ge(rstd_ready, n)
            for h in range(2):
                V.tensor_scalar(nbuf[:, i, half(h)], x[:, i, half(h)], rstd[:, i:i + 1], None,
                                ALU.mult).then_inc(n_ready, 1)

        def v_ffn(eng, f):
            u0 = U_FFN[f]

            def silu(i):
                eng.wait_ge(tanh_done, i + (f * NCH + 1))
                V.scalar_tensor_tensor(ffn_t, ffn_e, 1.0, bank[4][:, :], ALU.add, ALU.mult).then_inc(gate_read, 1)

            def hidden(i, up_unit):
                eng.wait_ge(unit_done, up_unit + 1)
                eng.wait_ge(gate_read, i + (f * NCH + 1))
                V.scalar_tensor_tensor(ffn_h, ffn_t, 0.5, bank[5][:, :], ALU.mult, ALU.mult).then_inc(up_read, 1)

            def low(i, buf=0):
                eng.wait_ge(h_rounded, i + (f * NCH + 1))
                V.tensor_tensor(h_lo[buf], ffn_h.rearrange("p (a b) -> p a b", a=2), h_hi[buf].bitcast(F32),
                                ALU.subtract).then_inc(h_ready, 1)

            v_split(eng, u0 + 2)
            silu(0)
            v_split(eng, u0 + 3)
            hidden(0, u0 + 1)
            low(0)
            with eng.Fori(1, NCH - 1) as i:
                unit = i * 3 + (u0 - 1)
                for j in range(3):
                    rest_unit(eng, unit + 2 + j, (u0 + 4 + j) % SLOTS)
                    if j == 0:
                        silu(i)
                    if j == 1:
                        hidden(i, unit + 1)
                low(i)
            unit = u0 + 3 * NCH - 4
            v_split(eng, unit + 2)
            silu(NCH - 1)
            v_split(eng, unit + 3)
            hidden(NCH - 1, unit + 1)
            low(NCH - 1, 1)
            v_split(eng, unit + 4)

        def v_mlp(eng):
            def square(i, fresh=False):
                eng.wait_ge(relu_done, i + 1)
                if not fresh:
                    eng.wait_ge(m_ready, i)
                V.scalar_tensor_tensor(ffn_h, bank[4][:, :], 0.0, ffn_e, ALU.max, ALU.mult).then_inc(sq_done, 1)

            def low(i, buf=0):
                eng.wait_ge(m_rounded, i + 1)
                V.tensor_tensor(h_lo[buf], ffn_h.rearrange("p (a b) -> p a b", a=2), h_hi[buf].bitcast(F32),
                                ALU.subtract).then_inc(m_ready, 1)

            v_split(eng, U_MLP + 2)
            square(0, True)
            low(0)
            with eng.Fori(0, (NCH2 - 1) // 3 - 1) as i:
                for j in range(3):
                    unit = i * 6 + (U_MLP + 1 + 2 * j)
                    nxt = U_MLP + 3 + 2 * j
                    rest_unit(eng, unit + 2, nxt % SLOTS)
                    square(i * 3 + (j + 1))
                    rest_unit(eng, unit + 3, (nxt + 1) % SLOTS)
                    low(i * 3 + (j + 1))
            for c in range(NCH2 - 3, NCH2):
                v_split(eng, U_MLP + 2 * c + 1)
                square(c)
                v_split(eng, U_MLP + 2 * c + 2)
                low(c, 1 if c == NCH2 - 1 else 0)

        def v_logits(eng, link, a):
            eng.wait_ge(scored, a + 1)
            if a:
                eng.wait_ge(exp_ready, a)
            if a >= A_DSA:
                for m in range(2):
                    last = V.tensor_tensor(logit[:, m, :], bank[2 * (a % 2) + m][:, 0:384], chosen, ALU.add)
                link(last)
            for m in range(2):
                slot = a if a < A_MOBA else 8 + 2 * (a - A_MOBA) + m if a < A_DSA else 2 * (a - A_DSA) + m
                for i in range(NT):
                    c = TILE_COLS[i]
                    src = logit[:, m, c] if a >= A_DSA else bank[2 * (a % 2) + m][:, c]
                    last = V.tensor_tensor_reduce(logit[:, m, c], src, table[:, slot, TABLE_COLS[i]], -SM, 3e38,
                                                  ALU.add, ALU.min, nmax[:, m, i:i + 1])
            last.then_inc(logits_read, 1)

        def v_probs(eng, link, a):
            eng.wait_ge(exp_ready, a + 1)
            if a:
                eng.wait_ge(turned, a)
            link(V.reciprocal(rz[:, :, :], zsum[:, :, :]))
            if a < A_MOBA:
                link(V.tensor_scalar(rz[:, 1, :], rz[:, 1, :], neg_lam[:, 0:1], None, ALU.mult))
            for m in range(1 if a < A_MOBA else 2):
                for i, c in enumerate(TILE_COLS):
                    last = V.tensor_scalar(prob[:, m, c], prob_e[:, m, c], rz[:, m, i:i + 1], None, ALU.mult)
            if a < A_MOBA:
                link(last)
                for i, c in enumerate(TILE_COLS):
                    last = V.scalar_tensor_tensor(prob[:, 0, c], prob_e[:, 1, c], rz[:, 1, i:i + 1], prob[:, 0, c],
                                                  ALU.mult, ALU.add)
            last.then_inc(prob_ready, 1)

        def v_out_step(eng, a):
            if a < A_MOBA:
                eng.wait_ge(applied, a + 1)
                V.tensor_copy(o1[:, :, a * VD:(a + 1) * VD],
                              bank[5][:, 0:SEQ].rearrange("p (a b) -> p a b", a=2)).then_inc(o_copied, 1)
            else:
                b, pr = (a - A_MOBA) // 4, (a - A_MOBA) % 4
                eng.wait_ge(o_squared, a + 1)
                V.tensor_tensor(y_lo[:, b, pr, :], bank[5][:, 0:SEQ], y_hi[:, b, pr, :].bitcast(F32),
                                ALU.subtract).then_inc(o_copied, 1)

        def v_dots(eng, link, g):
            for m in range(2):
                eng.wait_ge(dots_relu, 2 * g + m + 1)
                for i, c in enumerate(TILE_COLS):
                    w = wi_s[:, i, 2 * g + m:2 * g + m + 1]
                    if g == 0 and m == 0:
                        last = V.tensor_scalar(score[:, c], dots[:, m, c], w, None, ALU.mult)
                    else:
                        last = V.scalar_tensor_tensor(score[:, c], dots[:, m, c], w, score[:, c], ALU.mult, ALU.add)
                last.then_inc(dots_used, 1)
                eng.wait_ge(dots_used, 2 * g + m + 1)
            if g == 3:
                for i, c in enumerate(TILE_COLS):
                    last = V.scalar_tensor_tensor(work[:, c], score[:, c], IDX_SCALE, causal[:, TABLE_COLS[i]],
                                                  ALU.mult, ALU.add)
                link(last)

        def v_topk_round(eng, link):
            for i, c in enumerate(TILE_COLS):
                last = V.max(top8[:, i, :], work[:, c])
            link(last)
            for i, c in enumerate(TILE_COLS):
                last = V.match_replace(work[:, c], top8[:, i, :], work[:, c], TAKEN)
            link(last)

        def v_conv(eng, link, n):
            eng.wait_ge(proj_copied, COPIED[U_XC + 1] + 1)
            eng.wait_ge(set_done, 3)
            o = conv[:, n, :]
            link(V.tensor_scalar(o, xc[:, n, 3:259], col("conv_w_2", 12 + n), col("conv_b_2", n), ALU.mult, ALU.add))
            for tap in (2, 1, 0):
                ins = V.scalar_tensor_tensor(o, xc[:, n, tap:tap + 256], col("conv_w_2", 4 * tap + n), o,
                                             ALU.mult, ALU.add)
                if tap:
                    link(ins)
            ins.then_inc(conv_ready, 1)

        def v_mixer(eng, link):
            for unit, apply, score_step in TURNS:
                if score_step is not None:
                    if score_step == A_DSA:
                        eng.wait_ge(table2_in, 16 * 4)
                    v_logits(eng, link, score_step)
                v_split(eng, unit + 2)
                if score_step is not None:
                    v_probs(eng, link, score_step)
                if U_VA <= unit < U_MOBA:
                    v_dots(eng, link, unit - U_VA)
                if U_MOBA - 1 <= unit < U_MOBA - 1 + TOPK // 8:
                    v_topk_round(eng, link)
                if unit == U_MOBA - 2 + TOPK // 8:
                    link(V.tensor_scalar(chosen, work, -2e38, NEG, ALU.is_gt, ALU.mult))
                if U_DSA <= unit < U_DSA + CT:
                    v_conv(eng, link, unit - U_DSA)
                if apply is not None:
                    v_out_step(eng, apply)

        def v_gates(eng, link):
            for c in range(6):
                half, b = CHUNKS[c]
                for j in range(3):
                    v_split(eng, U_GATE + 3 * c + j + 2)
                    if 3 * c + j < CT:
                        g = gr[:, 3 * c + j, :]
                        eng.wait_ge(ri_act, 1)
                        link(V.tensor_scalar(g, g, 1.0, None, ALU.add))
                        V.reciprocal(g, g).then_inc(ri_sig, 1)
                    if (c, j) == (1, 1):
                        eng.wait_ge(gelu_sq, 1)
                        link(V.tensor_scalar(gl, gl, GELU_A, 1.0, ALU.mult, ALU.add))
                        V.tensor_tensor(gl, gl, yc, ALU.mult).then_inc(gelu_z, 1)
                    if (c, j) == (1, 2):
                        eng.wait_ge(ri_act, 2)
                        link(V.scalar_tensor_tensor(gi, gi, 1.0, conv, ALU.add, ALU.mult))
                    if (c, j) == (2, 0):
                        eng.wait_ge(lru_act, 1)
                        link(V.scalar_tensor_tensor(rt, rq, 1.0, rt, ALU.add, ALU.mult))
                        V.tensor_scalar(rt, rt, -4.0 * ROOT_MIN, None, ALU.min).then_inc(lru_u2, 1)
                    if (c, j) == (2, 1):
                        eng.wait_ge(gelu_t, 1)
                        link(V.scalar_tensor_tensor(yc, gl, 1.0, yc, ALU.add, ALU.mult))
                    if (c, j) == (3, 0):
                        eng.wait_ge(lru_root, 1)
                        link(V.tensor_tensor(rt, rt, gi, ALU.mult))
                        for n in range(CT):
                            last = V.tensor_tensor_scan(gr[:, n, :], ra[:, n, :], rt[:, n, :], 0.0, ALU.mult, ALU.add)
                        link(last)
                    if (c, j) == (3, 1):
                        V.scalar_tensor_tensor(yc, yc, 0.5, gr, ALU.mult, ALU.mult).then_inc(yc_ready, 1)
                    if (c, j) == (4, 0):
                        eng.wait_ge(yc_rounded, 1)
                        V.tensor_tensor(y_lo[:, 2], yc, y_hi[:, 2].bitcast(F32), ALU.subtract).then_inc(y_ready, 1)
                    if (c, j) == (5, 2):
                        v_merged_low(eng, 0)
                    if j == 2:
                        eng.wait_ge(unit_done, U_GATE + 3 * c + 3)
                        m = merged[:, 4 * half:4 * half + 4, :]
                        o = m if b == 0 else prod
                        eng.wait_ge(gate_act, 2 * c + 2)
                        for n in range(2):
                            last = V.scalar_tensor_tensor(
                                o[:, 2 * n:2 * n + 2, :], sig[:, 2 * n:2 * n + 2, :], 1.0,
                                bank[6 + n][:, :].rearrange("p (a b) -> p a b", a=2), ALU.add, ALU.mult)
                        last.then_inc(p_read, 1)
                        eng.wait_ge(p_read, c + 1)
                        if b:
                            ins = V.tensor_tensor(m, m, prod, ALU.add)
                            if b == 1:
                                link(ins)
                            else:
                                ins.then_inc(merged_ready, 1)

        @block.vector
        def _(eng):
            link = Link(eng, v_link)
            eng.wait_ge(small_in, SMALL)
            V.tensor_tensor(lprod, lp[:, 0:4:2], lp[:, 1:4:2], ALU.mult).then_inc(v_start, 1)
            eng.wait_ge(gb_in, 16)
            eng.wait_ge(pool_w_in, 16)
            for k in range(2):
                last = V.tensor_tensor(pool_w[:, :, k, :], pool_w[:, :, k, :],
                                       gb[:, 0, :].rearrange("p (g d) -> p g d", g=NG), ALU.mult)
            last.then_inc(pool_scaled, 1)
            eng.wait_ge(pe_start, 1)
            V.tensor_copy(par[:, :], bank[4][:, 0:NROWS]).then_inc(v_start, 1)
            eng.wait_ge(v_start, 2)
            lam = par[:, ROWS["lru_lambda_2"][0]:ROWS["lru_lambda_2"][0] + CT]
            link(V.tensor_scalar(sp[:, 0, :], lam, -1.0, None, ALU.mult))
            V.tensor_tensor(sp[:, 1, :], sp[:, 0, :], lam, ALU.max).then_inc(v_start, 1)
            eng.wait_ge(pe_start, 2)
            V.scalar_tensor_tensor(vec, bank[5][0:24, 0:384], 1.0 / SM, vecmask, ALU.mult, ALU.add).then_inc(v_start, 1)
            b0 = ROWS["b_r_2"][0]
            for m, k in ((0, -1.0), (1, 0.5)):
                V.tensor_scalar(gate_b[:, 4 * m:4 * m + 4], par[:, b0 + 4 * m:b0 + 4 * m + 4], k, None, ALU.mult)
            V.tensor_scalar(sub_gain[:, :], col("subln_g"), 1.0 - LAMBDA_INIT, None, ALU.mult)

            def pool_residual(i, h):
                eng.wait_ge(mixed, 2 * i + h + 1)
                link(V.scalar_tensor_tensor(x[:, i, half(h)], x[:, i, half(h)], ALPHA, acc[i][h],
                                            ALU.mult, ALU.add))

            for i in v_layernorm(eng, link, pool_residual, together=True):
                v_normalise(i)
            eng.wait_ge(lo_done, 1)
            v_transposed(eng, 0, 1, lambda k: col("ln_mix_g", k), lambda k: col("ln_mix_b", k))
            v_ffn(eng, 0)
            v_ln_phase(eng, link, 1, 0, U_V - 1, 1, "ln_ffn_g", "ln_ffn_b", 0)
            for j in range(4):
                v_split(eng, U_V + j + 2)
            eng.wait_ge(s_start, 2)
            link(V.scalar_tensor_tensor(sp[:, 0, :], sp[:, 0, :], 0.0, sp[:, 3, :], ALU.max, ALU.add))
            for k in range(2):
                V.tensor_scalar(lru_c[:, k * CT:(k + 1) * CT], sp[:, 0, :], -LRU_C * (k + 1), None, ALU.mult)
            link(V.tensor_tensor(neg_lam[:, :], e_lam[:, 1:2], e_lam[:, 0:1], ALU.subtract))
            link(V.tensor_scalar(neg_lam[:, :], neg_lam[:, :], LAMBDA_INIT, None, ALU.subtract))
            eng.wait_ge(table_in, 16 * 8)
            def v_prob_t(a):
                eng.wait_ge(turned, a + 1)
                if a:
                    eng.wait_ge(applied, a)
                V.tensor_copy(prob_t[:, 0, :], bank[6][:, 0:384]).then_inc(pt_copied, 1)

            by_head = [v[:, 0:2 * HEADS].rearrange("p (i h) -> p i h", i=NT) for v in (vareps, rstd)]

            def v_out_variance(h):
                eng.wait_ge(o_squared, 4 * h + 4)
                g = slice(4 * h, 4 * h + 4)
                V.tensor_scalar(by_head[0][:, :, g], sumsq[:, :, g], 1.0 / VD, LN_EPS,
                                ALU.mult, ALU.add).then_inc(var_ready, 1)
                var_count[0] += 1
                return var_count[0]

            def v_out_rows(h, n):
                eng.wait_ge(rstd_ready, n)
                eng.wait_ge(o_copied, 4 * h + 4)
                for i in range(NT):
                    o = o1[:, i, half(h)].rearrange("p (h v) -> p h v", h=4)
                    r = by_head[1][:, i, 4 * h:4 * h + 4].unsqueeze(2).broadcast_to([P, 4, VD])
                    V.tensor_tensor(o, o, r, ALU.mult).then_inc(n_ready, 1)

            for unit, apply, score_step in HEAD_TURNS[:-2]:
                if unit == U_HEAD + 6:
                    n = v_out_variance(0)
                if apply is not None:
                    v_prob_t(apply)
                if score_step is not None:
                    v_logits(eng, link, score_step)
                v_split(eng, unit + 2)
                if score_step is not None:
                    v_probs(eng, link, score_step)
                if unit == U_HEAD + 6:
                    v_out_rows(0, n)
                if apply is not None:
                    v_out_step(eng, apply)
            out_gain = lambda h: sub_gain[:, 0:1].broadcast_to([P, 4])
            v_tile1(eng, O_NORM, 0, out_gain)
            v_prob_t(HEADS - 2)
            for i in range(NT):
                v_low(eng, O_NORM, i, 0)
            v_logits(eng, link, HEADS - 1)
            v_out_step(eng, HEADS - 2)
            v_probs(eng, link, HEADS - 1)
            v_prob_t(HEADS - 1)
            v_out_step(eng, HEADS - 1)
            n = v_out_variance(1)
            v_split(eng, U_WO + 2)
            v_out_rows(1, n)
            v_low(eng, O_NORM, 0, 1)
            v_tile1(eng, O_NORM, 1, out_gain)
            v_low(eng, O_NORM, 1, 1)
            v_split(eng, U_WO + 3)
            v_split(eng, U_WO + 4)
            v_ln_phase(eng, link, 3, 1, U_FFN[1] - 1, 2, "ln_mix_g", "ln_mix_b", 1)
            v_ffn(eng, 1)
            eng.wait_ge(nat_ready, 3)
            eng.wait_ge(gb_in, 16 * 9)

            def centred(i):
                link(V.scalar_tensor_tensor(x[:, i, :], x[:, i, :], mv[:, i, 0:1], gb[:, 0, :],
                                            ALU.subtract, ALU.mult))

            n = []
            for i in v_layernorm(eng, link, lambda i, h: link(v_residual(eng, 2, U_QI, i, h, ALPHA)), centred,
                                 lambda: n.append(rms_variance(eng, link, 0, 0))):
                for h in range(2):
                    V.scalar_tensor_tensor(x[:, i, half(h)], x[:, i, half(h)], rstd[:, i:i + 1], gb[:, 1, half(h)],
                                           ALU.mult, ALU.add).then_inc(z_ready, 1)
            v_rms_rows(eng, 0, n[0])
            v_rms_rows(eng, 1, rms_variance(eng, link, 0, 1))
            v_transposed(eng, 4, U_QI + 1, lambda h: cols("norm_mix_g_2", 4 * h))
            v_mixer(eng, link)
            v_gates(eng, link)
            v_merged_low(eng, 1)
            for j in range(3):
                v_split(eng, U_WO2 + j + 2)
            for i in range(NT):
                for h in range(2):
                    v_residual(eng, 3, U_MLP, i, h, 1.0).then_inc(z_ready, 1)
                v_rms_rows(eng, i, rms_variance(eng, link, 1, i))
            v_transposed(eng, 5, U_MLP + 1, lambda h: cols("norm_mlp_g_2", 4 * h))
            v_mlp(eng)
            eng.wait_ge(gb_in, 16 * 10)
            for i in range(NT):
                for h in range(2):
                    v_residual(eng, 4, U_END, i, h, 1.0).then_inc(z_ready, 1)
                eng.wait_ge(rstd_ready, rms_variance(eng, link, 2, i))
                for h in range(2):
                    V.scalar_tensor_tensor(x[:, i, half(h)], x[:, i, half(h)], rstd[:, i:i + 1], gb[:, 0, half(h)],
                                           ALU.mult, ALU.mult).then_inc(out_ready, 1)

        @block.gpsimd
        def _(eng):
            G = nc.gpsimd

            def load_gb(*names_layers):
                for r, (name, k) in enumerate(names_layers):
                    src = t[name].rearrange("a b -> (a b)")[k * D:(k + 1) * D]
                    eng.dma_start(gb[:, r, :], src.partition_broadcast(P)).then_inc(gb_in, 16)

            def roots(n, cols, done):
                for _ in range(n):
                    at = slice(done[1], done[1] + cols) if n > 1 else slice(0, cols)
                    eng.wait_ge(var_ready, done[0] + 1)
                    G.tensor_tensor(rstd[:, at], vareps[:, at], minus_half[:, 0:1].broadcast_to([P, cols]), ALU.pow)\
                        .then_inc(rstd_ready, 1)
                    done[0] += 1
                    done[1] += cols

            done = [0, 0]

            def ln_roots():
                done[1] = 0
                roots(NT, 1, done)

            def natural(ev, loaded):
                eng.wait_ge(n_turned, 4 * ev + 4)
                eng.wait_ge(gb_in, loaded)
                for i in range(NT):
                    last = G.tensor_tensor(x[:, i, :], x[:, i, :], gb[:, 0, :], ALU.mult)
                last.then_inc(nat_link, 1)
                nat[0] += 1
                eng.wait_ge(nat_link, 2 * nat[0] - 1)
                for i in range(NT):
                    last = G.tensor_tensor(x[:, i, :], x[:, i, :], gb[:, 1, :], ALU.add)
                last.then_inc(nat_link, 1)
                eng.wait_ge(nat_link, 2 * nat[0])
                eng.sem_inc(nat_ready, 1)

            nat = [0]
            G.memset(ones, 1.0).then_inc(set_done, 1)
            G.memset(minus_half[:, :], -0.5).then_inc(set_done, 1)
            eng.wait_ge(x_in[0], 16)
            load_gb(("pool_scale", 0))
            eng.wait_ge(pool_scaled, 1)
            load_gb(("ln_mix_g", 0), ("ln_mix_b", 0))
            eng.wait_ge(hi_done, 1)
            G.tensor_tensor(w_lo[0][:, :], raw[0][:, :], w_hi[0][:, :].bitcast(F32), ALU.subtract).then_inc(lo_done, 1)
            ln_roots()
            natural(0, 48)
            load_gb(("ln_ffn_g", 0), ("ln_ffn_b", 0))
            eng.wait_ge(v_start, 4)
            for j in range(8):
                eng.wait_ge(unit_done, j + 1)
                r = slice(3 * j, 3 * j + 3)
                eng.dma_start(vec_dram[r], vec[r, :].unsqueeze(1).broadcast_to([3, P, 384])).then_inc(vec_out, 16)
            eng.wait_ge(vec_out, 16 * 8)

            def toeplitz(slot, head, n=2):
                src = bass.AP(vec_dram.tensor, vec_dram.offset + head * P * 384 + 127,
                              [[383, P], [P * 384, n], [1, SEQ]])
                return eng.dma_start(table[:, slot:slot + n, :], src)

            for j in range(8):
                eng.wait_ge(unit_done, 2 * j + 10)
                toeplitz(2 * j, 2 * j).then_inc(table_in, 16)
            eng.wait_ge(pe_start, 3)
            G.memset(wri, 0.0).then_inc(wri_zero, 1)
            eng.wait_ge(wri_zero, 1)
            for m, name in enumerate(("w_r_2", "w_i_2")):
                for e in range(2):
                    r = slice(e * DH, (e + 1) * DH)
                    eng.dma_start(wri[r, m, :, r], t[name][e:8:2].rearrange("n c d -> c n d")).then_inc(wri_in, 16)
            ln_roots()
            natural(1, 80)
            load_gb(("ln_mix_g", 1), ("ln_mix_b", 1))
            for h in range(2):
                v, r = (a[:, 0:2 * HEADS].rearrange("p (i h) -> p i h", i=NT)[:, :, 4 * h:4 * h + 4]
                        for a in (vareps, rstd))
                eng.wait_ge(var_ready, done[0] + 1)
                G.tensor_tensor(r, v, minus_half[:, 0:1].unsqueeze(2).broadcast_to([P, NT, 4]), ALU.pow)\
                    .then_inc(rstd_ready, 1)
                done[0] += 1
            eng.wait_ge(logits_read, HEADS)
            for j in range(4):
                eng.wait_ge(unit_done, U_WO + j)
                toeplitz(2 * j, 16 + 2 * j).then_inc(table2_in, 16)
            ln_roots()
            natural(3, 112)
            load_gb(("ln_ffn_g", 1), ("ln_ffn_b", 1))
            ln_roots()
            ln_roots()
            load_gb(("final_norm_g_2", 0))
            eng.wait_ge(x_ready, 10)
            G.memset(xc[:, :, 0:3], 0.0).then_inc(set_done, 1)
            ln_roots()
            ln_roots()


def kernel(**inputs):
    import concourse.bacc as bacc
    from concourse.bass_utils import run_bass_kernel_spmd

    nc = bacc.Bacc("TRN2", target_bir_lowering=False, num_devices=1)
    arrays = {k: np.ascontiguousarray(v) for k, v in inputs.items()}
    arrays.update(constants())
    t = {k: nc.dram_tensor(k, v.shape, mybir.dt.from_np(v.dtype), kind="ExternalInput").ap()
         for k, v in arrays.items()}
    for k in ("x", "pool_w", "w_qkv", "w_o", "lam_p", "w_in_2", "w_r_2", "w_i_2", "w_pa_2", "w_pb_2", "w_pc_2",
              "w_o_2", "w_up_2", "w_down_2", "conv_w_2"):
        t[k] = t[k][0]
    rows_of = dict(t)
    for k in ROWS:
        v = t[k]
        if len(v.shape) == 1:
            v = v.rearrange("(a b) -> a b", b=P)
        else:
            v = v.rearrange("a (c b) -> (a c) b", b=P)
        rows_of[k] = v
    rows_of["pool_scale"] = t["pool_scale"]
    rows_of["final_norm_g_2"] = t["final_norm_g_2"].rearrange("(a b) -> a b", a=1)
    out = nc.dram_tensor("out", (SEQ, D), F32, kind="ExternalOutput").ap()
    build(nc, rows_of, out)
    r = run_bass_kernel_spmd(nc, [arrays], core_ids=[0])
    return r.results[0]["out"].reshape(1, SEQ, D)
```
